# Optimizing a Trainium2 kernel written in Bass

```python
import jax, jax.numpy as jnp
from jax import lax
import numpy as np

D_MODEL = 2048
BATCH = 1
SEQ = 256
DEPTH = 1

HG_HEADS = 16
HG_EXPAND = 128
HG_KEY_DIM = HG_HEADS * HG_EXPAND
HG_VAL_DIM = 2048
HG_HEAD_V = HG_VAL_DIM // HG_HEADS
CHUNK = 64
CONV_DIM = 2048
CONV_WIDTH = 3
FFN_DIM = 5632
FFN_CONV_WIDTH = 3
EPS = 1e-6
F_MIN = 1e-30

SPLITS = (HG_KEY_DIM, HG_KEY_DIM, HG_VAL_DIM, HG_VAL_DIM,
          CONV_DIM, CONV_DIM, CONV_DIM,
          D_MODEL, D_MODEL)
IN_DIM = sum(SPLITS)

kernel_name = "hgrn2_shortconv_gated_hybrid"

def rms_norm(x, w):
    xf = x.astype(jnp.float32)
    y = xf * lax.rsqrt(jnp.mean(xf * xf, axis=-1, keepdims=True) + EPS)
    return (y * w.astype(jnp.float32)).astype(x.dtype)

def causal_dwconv(x, w, b=None):
    k_width, ch = w.shape
    y = lax.conv_general_dilated(
        x, w[:, None, :].astype(x.dtype), window_strides=(1,), padding=((k_width - 1, 0),),
        dimension_numbers=('NWC', 'WIO', 'NWC'), feature_group_count=ch)
    if b is not None:
        y = y + b.astype(x.dtype)
    return y

def _to_chunks(t):
    bsz, seq, heads, d = t.shape
    return t.reshape(bsz, seq // CHUNK, CHUNK, heads, d).transpose(1, 0, 3, 2, 4)

def hgrn2_recurrence(q, k, v, log_f):
    bsz, seq, heads, dk = q.shape
    dv = v.shape[-1]
    xs = (_to_chunks(q), _to_chunks(k), _to_chunks(v), _to_chunks(log_f))
    mask = jnp.tril(jnp.ones((CHUNK, CHUNK), dtype=bool))[:, :, None]

    def step(state, inp):
        qc, kc, vc, gc = inp
        b = jnp.cumsum(gc, axis=2)
        o_inter = jnp.einsum('bhtk,bhkv->bhtv', qc * jnp.exp(b), state)
        diff = b[:, :, :, None, :] - b[:, :, None, :, :]
        decay = jnp.where(mask, jnp.exp(jnp.where(mask, diff, 0.0)), 0.0)
        scores = jnp.einsum('bhtk,bhsk,bhtsk->bhts', qc, kc, decay)
        o_intra = jnp.einsum('bhts,bhsv->bhtv', scores, vc)
        b_last = b[:, :, -1:, :]
        new_state = (jnp.exp(b_last[:, :, 0, :])[..., None] * state
                     + jnp.einsum('bhsk,bhsv->bhkv', kc * jnp.exp(b_last - b), vc))
        return new_state, o_inter + o_intra

    s0 = jnp.zeros((bsz, heads, dk, dv), jnp.float32)
    _, ys = lax.scan(step, s0, xs)
    return ys.transpose(1, 0, 3, 2, 4).reshape(bsz, seq, heads, dv)

def setup_inputs(seed: int = 0) -> dict:
    key = jax.random.key(seed)
    ks = jax.random.split(key, 17)
    f32 = jnp.float32

    def nrm(k, shape, scale):
        return jax.random.normal(k, shape, f32) * scale

    def gain(k, shape):
        return 1.0 + 0.02 * jax.random.normal(k, shape, f32)

    return {
        "x": jax.random.normal(ks[0], (BATCH, SEQ, D_MODEL), f32),
        "norm_mix_pre": gain(ks[1], (DEPTH, D_MODEL)),
        "norm_mix_post": gain(ks[2], (DEPTH, D_MODEL)),
        "norm_ffn_pre": gain(ks[3], (DEPTH, D_MODEL)),
        "norm_ffn_post": gain(ks[4], (DEPTH, D_MODEL)),
        "w_in": nrm(ks[5], (DEPTH, D_MODEL, IN_DIM), D_MODEL ** -0.5),
        "hg_lower_bounds": nrm(ks[6], (DEPTH, HG_KEY_DIM), 0.1),
        "hg_out_norm": gain(ks[7], (DEPTH, HG_HEAD_V)),
        "w_hg_out": nrm(ks[8], (DEPTH, HG_VAL_DIM, D_MODEL), HG_VAL_DIM ** -0.5),
        "sc_conv": nrm(ks[9], (DEPTH, CONV_WIDTH, CONV_DIM), CONV_WIDTH ** -0.5),
        "w_sc_out": nrm(ks[10], (DEPTH, CONV_DIM, D_MODEL), CONV_DIM ** -0.5),
        "w_mix_out": nrm(ks[11], (DEPTH, D_MODEL, D_MODEL), D_MODEL ** -0.5),
        "w_ffn_up": nrm(ks[12], (DEPTH, D_MODEL, 2 * FFN_DIM), D_MODEL ** -0.5),
        "ffn_conv": nrm(ks[13], (DEPTH, FFN_CONV_WIDTH, 2 * FFN_DIM), FFN_CONV_WIDTH ** -0.5),
        "ffn_conv_bias": nrm(ks[14], (DEPTH, 2 * FFN_DIM), 0.02),
        "w_ffn_down": nrm(ks[15], (DEPTH, FFN_DIM, D_MODEL), FFN_DIM ** -0.5),
    }

def reference(x, norm_mix_pre, norm_mix_post, norm_ffn_pre, norm_ffn_post, w_in,
              hg_lower_bounds, hg_out_norm, w_hg_out, sc_conv, w_sc_out, w_mix_out,
              w_ffn_up, ffn_conv, ffn_conv_bias, w_ffn_down):
    bsz, seq, _ = x.shape
    lb_soft = jax.nn.softmax(hg_lower_bounds.astype(jnp.float32), axis=0)
    lower = jnp.cumsum(lb_soft, axis=0) - lb_soft[0]
    offsets = []
    acc = 0
    for s in SPLITS[:-1]:
        acc += s
        offsets.append(acc)

    for l in range(DEPTH):
        h = rms_norm(x, norm_mix_pre[l])
        proj = h @ w_in[l]
        q_r, f_r, i_r, g_r, cb, cc, ch, ga, gb = jnp.split(proj, offsets, axis=-1)

        lb = lower[l]
        z = f_r.astype(jnp.float32)
        sig = jax.nn.sigmoid(z)
        f_gate = lb + (1.0 - lb) * sig
        log_f = jnp.log(jnp.maximum(f_gate, F_MIN))
        k_in = (1.0 - lb) * (1.0 - sig)
        q_in = jax.nn.silu(q_r.astype(jnp.float32))
        shp_k = (bsz, seq, HG_HEADS, HG_EXPAND)
        o = hgrn2_recurrence(q_in.reshape(shp_k), k_in.reshape(shp_k),
                             i_r.astype(jnp.float32).reshape(bsz, seq, HG_HEADS, HG_HEAD_V),
                             log_f.reshape(shp_k))
        o = rms_norm(o, hg_out_norm[l]).reshape(bsz, seq, HG_VAL_DIM).astype(x.dtype)
        y_a = (o * jax.nn.silu(g_r)) @ w_hg_out[l]

        u = causal_dwconv(cc * ch, sc_conv[l])
        y_b = (cb * u) @ w_sc_out[l]

        mixed = jax.nn.sigmoid(ga) * y_a + jax.nn.sigmoid(gb) * y_b
        x = x + rms_norm(mixed @ w_mix_out[l], norm_mix_post[l])

        h = rms_norm(x, norm_ffn_pre[l])
        up = causal_dwconv(h @ w_ffn_up[l], ffn_conv[l], ffn_conv_bias[l])
        a, b = jnp.split(up, [FFN_DIM], axis=-1)
        y = (jax.nn.silu(a) * b) @ w_ffn_down[l]
        x = x + rms_norm(y, norm_ffn_post[l])
    return x


_drawn_inputs = setup_inputs


def setup_inputs(seed=0):
    import zlib

    import numpy as np

    out = dict(_drawn_inputs(seed))
    spreads = {}
    factors = {'norm_mix_post': 3.342,
     'norm_ffn_pre': 3.522,
     'norm_ffn_post': 4.956,
     'hg_out_norm': 6.328,
     'ffn_conv_bias': 3.484}
    for name, (base, spread) in spreads.items():
        noise = np.random.default_rng([zlib.crc32(name.encode()), seed]).standard_normal(out[name].shape)
        drawn = base * np.exp(spread * noise) if base else spread * noise
        out[name] = __import__('jax').numpy.asarray(drawn.astype(out[name].dtype))
    for name, factor in factors.items():
        out[name] = (out[name] * factor).astype(out[name].dtype)
    return out
```

```python
from contextlib import ExitStack, contextmanager

import numpy as np

import concourse.bass as bass
from concourse import mybir

P = 128
D_MODEL = 2048
T = 256
HEADS = 16
FFN = 5632
KT = D_MODEL // P
FT = FFN // P
CHUNK = 128
LEVELS = 7
EPS = 1e-6
F_MIN = 1e-30

SLAB = 8
RING = 4
LEAD = 3
COLS_MAIN = 9 * KT + 3 * KT + 2 * FT
SLABS_MAIN = COLS_MAIN * KT // SLAB
DOWN_SIZES = [SLAB] * (FT // SLAB) + [FT % SLAB]
DOWN_SLABS = len(DOWN_SIZES)

P_MIX_PRE, P_MIX_POST, P_FFN_PRE, P_FFN_POST, P_LOWER = (KT * n for n in range(5))
P_HEAD_NORM = 5 * KT
P_CONV = P_HEAD_NORM + 1
P_UPCONV = P_CONV + 3 * KT
P_UPBIAS = P_UPCONV + 3 * 2 * FT
N_PARAMS = P_UPBIAS + 2 * FT

F32 = mybir.dt.float32
F32R = mybir.dt.float32r
U8 = mybir.dt.uint8
ACT = mybir.ActivationFunctionType
ALU = mybir.AluOpType


class Tally:

    def __init__(self, n=0):
        self.n, self.trip = n, 0

    def add(self, k=1):
        self.n += k
        return self.value()

    def value(self):
        return self.trip + self.n


@contextmanager
def repeat(eng, trips, per_trip):
    before = {t: t.n for t in per_trip}
    with eng.Fori(0, trips) as i:
        for t, k in per_trip.items():
            t.trip = i * k
        yield i
    for t, k in per_trip.items():
        assert t.n - before[t] == k, (t.n - before[t], k)
        t.trip = 0
        t.n += k * (trips - 1)


def at(i, c=1):
    return bass.ds(i, c)


def build(nc, xT, params, ident_d, masks_d, w_main, w_down, outT):
    ctx = ExitStack()
    with ctx:
        BASE = 16512
        KB = 1024

        def sb(name, shape, dt, off):
            return nc.alloc_sbuf_tensor_at(name, [P] + shape, dt, offset=BASE + off)

        tile_b = T * 4
        act_b = KT * tile_b
        norm_h = sb("norm_h", [KT, T], F32R, 0)
        norm_l = sb("norm_l", [KT, T], F32R, act_b)
        down_out = sb("down_out", [KT, T], F32, 0)
        conv_h = sb("conv_h", [KT, T], F32R, 32 * KB)
        conv_l = sb("conv_l", [KT, T], F32R, 48 * KB)
        heads_h = sb("heads_h", [KT, T], F32R, 32 * KB)
        heads_l = sb("heads_l", [KT, T], F32R, 48 * KB)
        mix_out = sb("mix_out", [KT, T], F32, 32 * KB)
        head_o = sb("head_o", [HEADS, T], F32, 64 * KB)
        masks_f = sb("masks_f", [LEVELS, 2, CHUNK // 2], F32, 64 * KB)
        head_g = sb("head_g", [HEADS, T], F32, 80 * KB)
        mixed_h = sb("mixed_h", [KT, T], F32R, 64 * KB)
        mixed_l = sb("mixed_l", [KT, T], F32R, 80 * KB)
        conv_part = sb("conv_part", [KT, T], F32, 96 * KB)
        gate_a = sb("gate_a", [KT, T], F32, 112 * KB)
        hid_h = sb("hid_h", [FT, T], F32R, 32 * KB)
        hid_l = sb("hid_l", [FT, T], F32R, 76 * KB)
        x = sb("x", [KT, T], F32, 128 * KB)
        raw = [sb(f"raw{s}", [SLAB, P], F32, (144 + 4 * s) * KB) for s in range(RING)]
        high = [sb(f"high{s}", [SLAB, P], F32R, (160 + 4 * s) * KB) for s in range(RING)]
        low = [sb(f"low{s}", [SLAB, P], F32R, (176 + 4 * s) * KB) for s in range(RING)]
        off = 192 * KB
        par = sb("par", [N_PARAMS], F32, off); off += -(-N_PARAMS * 4 // 32) * 32
        ident = sb("ident", [P], F32, off); off += P * 4
        ones = sb("ones", [P], F32, off); off += P * 4
        masks = sb("masks", [LEVELS, 2, CHUNK // 2], U8, off); off += LEVELS * CHUNK
        eps = sb("eps", [1], F32, off); off += 32
        lower = sb("lower", [KT], F32, off); off += KT * 4
        upper = sb("upper", [KT], F32, off); off += KT * 4
        neg_upper = sb("neg_upper", [KT], F32, off); off += KT * 4
        head_r = sb("head_r", [2, HEADS], F32, off); off += 2 * HEADS * 4
        G = off
        slot = tile_b + 32
        assert BASE + G + 10 * slot <= 229344, BASE + G + 10 * slot

        def work(name, n, dt=F32, cols=T):
            return sb(name, [cols], dt, G + n * slot)

        ch_cc = work("ch_cc", 0, cols=T + 2)
        cc = work("cc", 1)
        conv_u = work("conv_u", 2)
        conv_y = work("conv_y", 3)
        gate_b = work("gate_b", 4)
        square = [work("square0", 5), work("square1", 6)]
        square_sum = work("square_sum", 7)
        root = work("root", 8)
        rstd = work("rstd", 9)
        scaled = [work("scaled0", 3), work("scaled1", 4)]
        diag = [sb(f"diag{n}", [2, P], F32, G + n * slot) for n in range(2)]
        blend = work("blend", 2)
        blend2 = work("blend2", 3)
        up_a = work("up_a", 0)
        up_b = work("up_b", 1)
        silu_a = work("silu_a", 2)
        hidden = work("hidden", 3)

        R = 32 * KB
        def rec(name, n, shape):
            return sb(name, shape, F32, R + n * KB)
        f_sig = rec("f_sig", 0, [T])
        f_gate = rec("f_gate", 1, [T])
        key = rec("key", 2, [T])
        q_sig = rec("q_sig", 3, [T])
        query = rec("query", 4, [T])
        q_run = rec("q_run", 5, [T])
        k_run = rec("k_run", 6, [T])
        v_chan = rec("v_chan", 7, [T])
        g_sig = rec("g_sig", 8, [T])
        totals = rec("totals", 9, [T])
        v_tok = rec("v_tok", 10, [2, P])
        o_square = rec("o_square", 11, [T])
        scores = rec("scores", 12, [3, CHUNK])

        acc = [nc.alloc_psum_tensor(f"acc{n}", [P, 512], F32) for n in range(4)]
        level_ps = nc.alloc_psum_tensor("level_ps", [P, 512], F32)
        o_ps = nc.alloc_psum_tensor("o_ps", [P, 512], F32)
        v_ps = nc.alloc_psum_tensor("v_ps", [P, 512], F32)
        stat_ps = nc.alloc_psum_tensor("stat_ps", [P, 512], F32)
        bcast_ps = [level_ps, o_ps]

        def sem(name):
            return nc.alloc_semaphore(name)

        x_loaded = [sem(f"x_loaded{n}") for n in range(4)]
        consts_loaded = sem("consts_loaded")
        raw_loaded = [sem(f"raw_loaded{s}") for s in range(RING)]
        high_ready = sem("high_ready")
        low_ready = sem("low_ready")
        slabs_used = sem("slabs_used")
        acc_read = [sem(f"acc_read{n}") for n in range(4)]
        vec_step = sem("vec_step")
        bound_shifted = sem("bound_shifted")
        bound_exp = sem("bound_exp")
        consts_made = sem("consts_made")
        squares_made = sem("squares_made")
        squares_read = sem("squares_read")
        sums_made = sem("sums_made")
        root_made = sem("root_made")
        rstd_made = sem("rstd_made")
        resid_made = sem("resid_made")
        normed = sem("normed")
        conv_ready = sem("conv_ready")
        gates_read = sem("gates_read")
        q_sig_ready = sem("q_sig_ready")
        g_sig_ready = sem("g_sig_ready")
        k_run_ready = sem("k_run_ready")
        q_run_ready = sem("q_run_ready")
        level_scored = sem("level_scored")
        level_merged = sem("level_merged")
        v_transposed = sem("v_transposed")
        v_ready = sem("v_ready")
        o_made = sem("o_made")
        o_squared = sem("o_squared")
        head_summed = sem("head_summed")
        diag_ready = sem("diag_ready")
        head_bcast = sem("head_bcast")
        head_scaled = sem("head_scaled")
        heads_high = sem("heads_high")
        heads_ready = sem("heads_ready")
        mixed_ready = sem("mixed_ready")
        tap_ready = sem("tap_ready")
        silu_ready = sem("silu_ready")
        hidden_read = sem("hidden_read")
        hidden_ready = sem("hidden_ready")
        out_made = sem("out_made")
        stored = sem("stored")

        block = ctx.enter_context(nc.Block())

        @block.sync
        def _(sp):
            for n in range(4):
                sp.dma_start(x[:, 4 * n:4 * n + 4, :], xT[:, 4 * n:4 * n + 4, :]).then_inc(x_loaded[n], 16)
            sp.dma_start(par[:], params).then_inc(consts_loaded, 16)
            sp.dma_start(ident[:], ident_d).then_inc(consts_loaded, 16)
            sp.dma_start(masks_f[:], masks_d).then_inc(consts_loaded, 16)
            freed = Tally(0)
            with repeat(sp, SLABS_MAIN // RING, {freed: RING}) as i:
                for s in range(RING):
                    sp.wait_ge(low_ready, freed.add())
                    sp.dma_start(raw[s][:], w_main[at(i * RING + s), :, :, :].rearrange("o p k c -> p (o k) c")
                                 ).then_inc(raw_loaded[s], 16)
            with repeat(sp, KT // 2, {freed: 2 * DOWN_SLABS}) as i:
                for m in range(2 * DOWN_SLABS):
                    n = m % DOWN_SLABS
                    sp.wait_ge(low_ready, freed.add())
                    sp.dma_start(raw[m % RING][:, 0:DOWN_SIZES[n], :],
                                 w_down[at(2 * i + m // DOWN_SLABS), :, n * SLAB:n * SLAB + DOWN_SIZES[n], :]
                                 .rearrange("o p k c -> p (o k) c")).then_inc(raw_loaded[m % RING], 16)
            for n in range(4):
                sp.wait_ge(out_made, 4 * n + 4)
                sp.dma_start(outT[:, 4 * n:4 * n + 4, :], down_out[:, 4 * n:4 * n + 4, :]).then_inc(stored, 16)
            sp.wait_ge(stored, 64)

        @block.scalar
        def _(act):
            slabs = Tally()
            loads = [Tally() for _ in range(RING)]
            cols = Tally(RING)
            reads = [Tally(1) for _ in range(4)]
            squares = Tally(2)
            gates, sums, levels, decays, outs, vts = Tally(1), Tally(), Tally(), Tally(), Tally(), Tally()

            def split(n, size=SLAB):
                s = n % RING
                act.wait_ge(raw_loaded[s], loads[s].add(16))
                act.wait_ge(slabs_used, slabs.add())
                nc.scalar.activation(high[s][:, 0:size, :], raw[s][:, 0:size, :], ACT.Copy).then_inc(high_ready, 1)

            def finished(slot, n=2, wait=True):
                v = cols.add(n)
                if wait:
                    act.wait_ge(slabs_used, v)
                reads[slot].add()

            def loop(trips, n_cols, slots, more=None):
                n = 2 * n_cols
                per = {slabs: n, cols: n, squares: 0}
                for s in range(RING):
                    per[loads[s]] = 16 * n // RING
                for s in range(4):
                    per[reads[s]] = slots.count(s)
                per.update(more or {})
                return repeat(act, trips, per)

            def root_of(ps, out, scale):
                act.wait_ge(sums_made, sums.add())
                nc.scalar.activation(out, ps, ACT.Sqrt, bias=eps[:], scale=scale).then_inc(root_made, 1)

            act.wait_ge(consts_made, 2)
            for k in range(KT):
                if k % 4 == 0:
                    act.wait_ge(x_loaded[k // 4], 16)
                act.wait_ge(squares_read, squares.value() - 1)
                squares.add()
                nc.scalar.activation(square[k % 2][:], x[:, k, :], ACT.Square).then_inc(squares_made, 1)
            root_of(stat_ps[:, 0:T], root[:], 1.0 / D_MODEL)
            for n in range(LEAD):
                split(n)
            act.wait_ge(bound_shifted, 1)
            nc.scalar.activation(neg_upper[:], lower[:], ACT.Exp).then_inc(bound_exp, 1)

            with loop(KT // 2, 6, [0, 1, 2] * 2) as i:
                for c in range(6):
                    split(2 * c + LEAD)
                    split(2 * c + LEAD + 1)
                    finished(c % 3, wait=c % 3 == 0)
                    if c % 3 == 0:
                        act.wait_ge(acc_read[1], reads[1].value())
                        nc.scalar.activation(cc[:], acc[0][:, 0:T], ACT.Copy).then_inc(acc_read[0], 1)

            with loop(KT, 2, [0, 1]) as j:
                split(LEAD)
                split(LEAD + 1)
                finished(0)
                act.wait_ge(acc_read[1], reads[1].value())
                nc.scalar.activation(gate_b[:], acc[0][:, 0:T], ACT.Sigmoid).then_inc(acc_read[0], 1)
                split(LEAD + 2)
                split(LEAD + 3)
                finished(1, wait=False)

            def head_extra_a(out_on):
                if out_on:
                    act.wait_ge(o_made, outs.add())
                    nc.scalar.activation(o_square[:], o_ps[:, 0:T], ACT.Square).then_inc(o_squared, 1)

            def head_extra_b(levels_on):
                if levels_on:
                    act.wait_ge(v_transposed, vts.add())
                    nc.scalar.activation(v_tok[:], v_ps[:, 0:T].rearrange("p (a b) -> p a b", a=2),
                                         ACT.Copy).then_inc(v_ready, 1)

            def head(levels_on, out_on):
                split(LEAD)
                head_extra_a(out_on)
                split(LEAD + 1)
                head_extra_b(levels_on)
                finished(0)
                act.wait_ge(gates_read, gates.value())
                gates.add()
                nc.scalar.activation(f_sig[:], acc[0][:, 0:T], ACT.Sigmoid).then_inc(acc_read[0], 1)
                split(LEAD + 2)
                split(LEAD + 3)
                finished(1)
                nc.scalar.activation(q_sig[:], acc[1][:, 0:T], ACT.Sigmoid).then_inc(q_sig_ready, 1)
                split(LEAD + 4)
                split(LEAD + 5)
                finished(2)
                nc.scalar.activation(v_chan[:], acc[2][:, 0:T], ACT.Copy).then_inc(acc_read[2], 1)
                split(LEAD + 6)
                split(LEAD + 7)
                finished(3)
                nc.scalar.activation(g_sig[:], acc[3][:, 0:T], ACT.Sigmoid).then_inc(g_sig_ready, 1)
                act.wait_ge(gates_read, gates.value())
                if levels_on:
                    act.wait_ge(level_scored, levels.add(LEVELS + 1))
                nc.scalar.activation(k_run[:], key[:], ACT.Copy).then_inc(k_run_ready, 1)

            head(False, False)
            head(True, False)
            with loop(HEADS - 2, 4, [0, 1, 2, 3], {gates: 1, levels: LEVELS + 1, outs: 1, vts: 1}):
                head(True, True)

            def gate_tile(slot, j):
                finished(slot)
                nc.scalar.activation(gate_a[:, at(j), :].rearrange("p a t -> p (a t)"), acc[slot][:, 0:T],
                                     ACT.Sigmoid).then_inc(acc_read[slot], 1)

            for c in range(4):
                split(2 * c + LEAD)
                if c == 0:
                    head_extra_a(True)
                split(2 * c + LEAD + 1)
                if c == 0:
                    head_extra_b(True)
                gate_tile(c, c)
            split(LEAD)
            head_extra_a(True)
            split(LEAD + 1)
            gate_tile(0, 4)
            split(LEAD + 2)
            split(LEAD + 3)
            gate_tile(1, 5)
            act.wait_ge(head_summed, HEADS)
            nc.scalar.activation(head_r[:], stat_ps[:, 0:2 * HEADS].rearrange("p (a b) -> p a b", a=2),
                                 ACT.Sqrt, bias=eps[:], scale=1.0 / P).then_inc(root_made, 1)
            scaleds = Tally(HEADS)
            with loop(4, 2, [0, 1], {scaleds: 4}) as i:
                for c in range(2):
                    for b in range(2):
                        split(2 * c + b + LEAD)
                        h = 2 * c + b
                        if c == 0 and b == 0:
                            act.wait_ge(rstd_made, 2)
                        for half in range(2):
                            done = nc.scalar.activation(diag[h % 2][:, half, :], ident[:], ACT.Copy,
                                                        scale=head_r[:, half, at(4 * i + h)])
                        done.then_inc(diag_ready, 1)
                        act.wait_ge(head_scaled, scaleds.add())
                        nc.scalar.activation(heads_h[:, at(4 * i + h), :].rearrange("p a t -> p (a t)"),
                                             scaled[h % 2][:], ACT.Copy).then_inc(heads_high, 1)
                    gate_tile(c, 2 * i + 6 + c)
            for c in range(2):
                split(2 * c + LEAD)
                split(2 * c + LEAD + 1)
                gate_tile(c, 14 + c)

            with loop(KT // 2, 2, [0, 1]):
                for c in range(2):
                    split(2 * c + LEAD)
                    split(2 * c + LEAD + 1)
                    finished(c, wait=False)

            def out_tile(dst, slot, j):
                act.wait_ge(squares_read, squares.value() - 1)
                squares.add()
                nc.scalar.activation(square[slot][:], acc[slot][:, 0:T], ACT.Square).then_inc(squares_made, 1)
                nc.scalar.activation(dst[:, at(j), :].rearrange("p a t -> p (a t)"), acc[slot][:, 0:T], ACT.Copy
                                     ).then_inc(acc_read[slot], 1)

            with loop(KT // 2, 2, [0, 1], {squares: 2}) as i:
                for c in range(2):
                    split(2 * c + LEAD)
                    split(2 * c + LEAD + 1)
                    finished(c)
                    out_tile(mix_out, c, 2 * i + c)
            root_of(stat_ps[:, 0:T], root[:], 1.0 / D_MODEL)
            resid = Tally()
            with repeat(act, KT // 2, {resid: 2, squares: 2}) as i:
                for c in range(2):
                    act.wait_ge(resid_made, resid.add())
                    act.wait_ge(squares_read, squares.value() - 1)
                    squares.add()
                    nc.scalar.activation(square[c][:], x[:, at(2 * i + c), :].rearrange("p a t -> p (a t)"),
                                         ACT.Square).then_inc(squares_made, 1)
            root_of(stat_ps[:, 0:T], root[:], 1.0 / D_MODEL)

            used = Tally(1)
            with loop(FT, 2, [0, 1], {used: 1}) as j:
                for c, dst in enumerate((up_a, up_b)):
                    split(2 * c + LEAD)
                    split(2 * c + LEAD + 1)
                    finished(c)
                    if c == 0:
                        act.wait_ge(hidden_read, used.value())
                        used.add()
                    nc.scalar.activation(dst[:], acc[c][:, 0:T], ACT.Identity,
                                         bias=par[:, at(j + (P_UPBIAS + c * FT))],
                                         scale=par[:, at(j + (P_UPCONV + 4 * FT + c * FT))]).then_inc(tap_ready, 1)
                act.wait_ge(acc_read[0], reads[0].value())
                nc.scalar.activation(silu_a[:], up_a[:], ACT.Silu).then_inc(silu_ready, 1)

            per = {slabs: 2 * DOWN_SLABS, cols: 2 * DOWN_SLABS, reads[0]: 1, reads[1]: 1, squares: 2}
            for s in range(RING):
                per[loads[s]] = 16 * 2 * DOWN_SLABS // RING

            def down_pair(i, last):
                for c in range(2):
                    for n in range(DOWN_SLABS):
                        m = c * DOWN_SLABS + n + LEAD
                        if not last or m < 2 * DOWN_SLABS:
                            split(m, DOWN_SIZES[m % DOWN_SLABS])
                    finished(c, DOWN_SLABS)
                    out_tile(down_out, c, 2 * i + c)
            with repeat(act, KT // 2 - 1, per) as i:
                down_pair(i, False)
            down_pair(KT // 2 - 1, True)
            root_of(stat_ps[:, 0:T], root[:], 1.0 / D_MODEL)

        @block.vector
        def _(dve):
            slabs = Tally()
            cols = Tally(RING)
            reads = [Tally(1) for _ in range(4)]
            steps = Tally()
            (squares, roots, qs, gs, krs, scored, outs, bcasts, highs, taps, silus) = (Tally() for _ in range(11))

            def step(ins):
                ins.then_inc(vec_step, 1)
                return steps.add()

            def split(n, size=SLAB):
                s = n % RING
                dve.wait_ge(high_ready, slabs.add())
                nc.vector.tensor_tensor(low[s][:, 0:size, :], raw[s][:, 0:size, :], high[s][:, 0:size, :].bitcast(F32),
                                        ALU.subtract).then_inc(low_ready, 1)

            def finished(slot, n=2, wait=True):
                v = cols.add(n)
                if wait:
                    dve.wait_ge(slabs_used, v)
                return reads[slot].add()

            def loop(trips, n_cols, slots, more=None):
                per = {slabs: 2 * n_cols, cols: 2 * n_cols}
                for s in range(4):
                    per[reads[s]] = slots.count(s)
                per.update(more or {})
                return repeat(dve, trips, per)

            def flat(t, i):
                return t[:, at(i), :].rearrange("p a t -> p (a t)")

            def reciprocal_root():
                dve.wait_ge(root_made, roots.add())
                nc.vector.reciprocal(rstd[:], root[:]).then_inc(rstd_made, 1)

            norms = Tally()

            def norm(gain):
                with repeat(dve, KT // 2, {steps: 4, norms: 2}) as i:
                    for c in range(2):
                        v = step(nc.vector.scalar_tensor_tensor(scaled[c][:], flat(x, 2 * i + c),
                                                                par[:, at(2 * i + (gain + c))], rstd[:],
                                                                ALU.mult, ALU.mult))
                    dve.wait_ge(vec_step, v)
                    for c in range(2):
                        v = step(nc.vector.tensor_copy(flat(norm_h, 2 * i + c), scaled[c][:]))
                    dve.wait_ge(vec_step, v)
                    for c in range(2):
                        nc.vector.tensor_tensor(flat(norm_l, 2 * i + c), scaled[c][:],
                                                flat(norm_h, 2 * i + c).bitcast(F32),
                                                ALU.subtract).then_inc(normed, 1)
                    dve.wait_ge(normed, norms.add(2))

            dve.sem_inc(low_ready, RING)
            for s in range(4):
                dve.sem_inc(acc_read[s], 1)
            dve.sem_inc(squares_read, 2)
            dve.sem_inc(gates_read, 1)
            dve.sem_inc(hidden_read, 1)
            nc.vector.memset(ones[:], 1.0).then_inc(consts_made, 1)
            nc.vector.memset(eps[:], EPS).then_inc(consts_made, 1)
            step(nc.vector.memset(square_sum[:], 0.0))
            step(nc.vector.memset(ch_cc[:, 0:2], 0.0))
            dve.wait_ge(consts_loaded, 48)
            lb = par[:, P_LOWER:P_LOWER + KT]
            step(nc.vector.tensor_copy(masks[:], masks_f[:]))
            nc.vector.tensor_tensor(lower[:], lb, lb, ALU.subtract).then_inc(bound_shifted, 1)

            reciprocal_root()
            dve.wait_ge(rstd_made, 1)
            norm(P_MIX_PRE)
            for n in range(LEAD):
                split(n)
            dve.wait_ge(bound_exp, 1)
            dve.wait_ge(vec_step, step(nc.vector.reciprocal(upper[:], neg_upper[:])))
            dve.wait_ge(vec_step, step(nc.vector.tensor_tensor(neg_upper[:], neg_upper[:], upper[:], ALU.mult)))
            dve.wait_ge(vec_step, step(nc.vector.tensor_tensor(lower[:], neg_upper[:], neg_upper[:], ALU.subtract)))
            step(nc.vector.tensor_scalar(upper[:], lower[:], -1.0, 1.0, ALU.mult, ALU.add))
            dve.wait_ge(vec_step, step(nc.vector.tensor_scalar(neg_upper[:], lower[:], -1.0, None, ALU.add)))

            with loop(KT // 2, 6, [0, 1, 2] * 2, {steps: 8}) as i:
                for h in range(2):
                    j = 2 * i + h
                    base = 6 * h
                    split(base + LEAD)
                    split(base + LEAD + 1)
                    cc_read = finished(0, wait=False)
                    split(base + LEAD + 2)
                    split(base + LEAD + 3)
                    v = finished(1)
                    dve.wait_ge(acc_read[0], cc_read)
                    nc.vector.tensor_tensor(ch_cc[:, 2:T + 2], acc[1][:, 0:T], cc[:], ALU.mult).then_inc(acc_read[1], 1)
                    dve.wait_ge(acc_read[1], v)
                    tap = [par[:, at(j + (P_CONV + n * KT))] for n in range(3)]
                    dve.wait_ge(vec_step, step(nc.vector.tensor_scalar(conv_u[:], ch_cc[:, 2:T + 2], tap[2], None, ALU.mult)))
                    dve.wait_ge(vec_step, step(nc.vector.scalar_tensor_tensor(conv_u[:], ch_cc[:, 1:T + 1], tap[1],
                                                                              conv_u[:], ALU.mult, ALU.add)))
                    step(nc.vector.scalar_tensor_tensor(conv_u[:], ch_cc[:, 0:T], tap[0], conv_u[:], ALU.mult, ALU.add))
                    split(base + LEAD + 4)
                    split(base + LEAD + 5)
                    v = finished(2)
                    dve.wait_ge(vec_step, steps.value())
                    nc.vector.tensor_tensor(conv_y[:], acc[2][:, 0:T], conv_u[:], ALU.mult).then_inc(acc_read[2], 1)
                    dve.wait_ge(acc_read[2], v)
                    dve.wait_ge(vec_step, step(nc.vector.tensor_copy(flat(conv_h, j), conv_y[:])))
                    nc.vector.tensor_tensor(flat(conv_l, j), conv_y[:], flat(conv_h, j).bitcast(F32),
                                            ALU.subtract).then_inc(conv_ready, 1)

            with loop(KT, 2, [0, 1]) as j:
                split(LEAD)
                split(LEAD + 1)
                g = finished(0, wait=False)
                split(LEAD + 2)
                split(LEAD + 3)
                finished(1)
                dve.wait_ge(acc_read[0], g)
                nc.vector.tensor_tensor(flat(conv_part, j), acc[1][:, 0:T], gate_b[:], ALU.mult).then_inc(acc_read[1], 1)

            def total(level):
                if level == 0:
                    return f_gate[:]
                start = T - 2 * (T >> level)
                return totals[:, start:start + (T >> level)]

            def halves(t, h):
                return t[:].rearrange("p (b u h) -> p b u h", u=2, h=h)

            def merge(s):
                dve.wait_ge(level_scored, scored.add())
                if s == LEVELS:
                    nc.vector.tensor_copy(scores[:, 1, :], level_ps[:, 0:CHUNK]).then_inc(level_merged, 1)
                    return
                h = 1 << s
                if s == 0:
                    dve.wait_ge(k_run_ready, krs.add())
                    v = step(nc.vector.tensor_tensor(
                        scores[:, 0:3:2, :], level_ps[:, CHUNK:3 * CHUNK].rearrange("p (c t) -> p c t", c=2),
                        ident[:].rearrange("p (o t) -> p o t", o=1).broadcast_to([P, 2, CHUNK]), ALU.mult))
                tot = total(s).rearrange("p (b u o) -> p b u o", u=2, o=1)
                nb = T // (2 * h)
                nc.vector.tensor_tensor(halves(q_run, h)[:, :, 1, :], halves(q_run, h)[:, :, 1, :],
                                        tot[:, :, 0, :].broadcast_to([P, nb, h]), ALU.mult)
                nc.vector.tensor_tensor(halves(k_run, h)[:, :, 0, :], halves(k_run, h)[:, :, 0, :],
                                        tot[:, :, 1, :].broadcast_to([P, nb, h]), ALU.mult)
                if s == 0:
                    dve.wait_ge(vec_step, v)
                if s < LEVELS - 1:
                    t2 = total(s).rearrange("p (b u) -> p b u", u=2)
                    nc.vector.tensor_tensor(total(s + 1), t2[:, :, 0], t2[:, :, 1], ALU.mult)
                nc.vector.copy_predicated(
                    scores[:, 0:3:2, :].rearrange("p c (b u h) -> p c b u h", u=2, h=h)[:, :, :, 1, :],
                    masks[:, s, :, :].rearrange("p c (b h) -> p c b h", h=h),
                    level_ps[:, 0:CHUNK].rearrange("p (c b h) -> p c b h", c=2, h=h)).then_inc(level_merged, 1)

            def head_output(i):
                dve.wait_ge(o_squared, outs.add())
                nc.vector.tensor_tensor(flat(head_o, i), o_ps[:, 0:T], flat(head_g, i), ALU.mult).then_inc(head_scaled, 1)

            def head(i, levels_on, out_on):
                split(LEAD)
                if out_on:
                    head_output(i - 2)
                if levels_on:
                    merge(0)
                split(LEAD + 1)
                if levels_on:
                    merge(1)
                v = finished(0, wait=False)
                dve.wait_ge(acc_read[0], v)
                dve.wait_ge(vec_step, step(nc.vector.tensor_scalar(f_gate[:], f_sig[:], upper[:, at(i)], lower[:, at(i)],
                                                                   ALU.mult, ALU.add)))
                step(nc.vector.tensor_scalar(f_gate[:], f_gate[:], F_MIN, None, ALU.max))
                nc.vector.tensor_scalar(key[:], f_sig[:], -1.0, neg_upper[:, at(i)], ALU.add, ALU.mult).then_inc(gates_read, 1)
                split(LEAD + 2)
                if levels_on:
                    merge(2)
                split(LEAD + 3)
                if levels_on:
                    merge(3)
                vq = finished(1, wait=False)
                dve.wait_ge(q_sig_ready, qs.add())
                nc.vector.tensor_tensor(query[:], acc[1][:, 0:T], q_sig[:], ALU.mult).then_inc(acc_read[1], 1)
                split(LEAD + 4)
                if levels_on:
                    merge(4)
                split(LEAD + 5)
                if levels_on:
                    merge(5)
                finished(2, wait=False)
                split(LEAD + 6)
                if levels_on:
                    merge(6)
                split(LEAD + 7)
                if levels_on:
                    merge(7)
                finished(3, wait=False)
                dve.wait_ge(g_sig_ready, gs.add())
                nc.vector.scalar_tensor_tensor(flat(head_g, i), acc[3][:, 0:T], par[:, P_HEAD_NORM:P_HEAD_NORM + 1],
                                               g_sig[:], ALU.mult, ALU.mult).then_inc(acc_read[3], 1)
                dve.wait_ge(acc_read[1], vq)
                dve.wait_ge(vec_step, steps.value())
                nc.vector.tensor_tensor(q_run[:], query[:], f_gate[:], ALU.mult).then_inc(q_run_ready, 1)

            head(0, False, False)
            head(1, True, False)
            with loop(HEADS - 2, 4, [0, 1, 2, 3],
                      {steps: 3, scored: LEVELS + 1, krs: 1, qs: 1, gs: 1, outs: 1}) as i:
                head(i + 2, True, True)

            for c in range(4):
                split(2 * c + LEAD)
                if c == 0:
                    head_output(HEADS - 2)
                merge(2 * c)
                split(2 * c + LEAD + 1)
                merge(2 * c + 1)
                finished(c, wait=False)
            split(LEAD)
            head_output(HEADS - 1)
            split(LEAD + 1)
            finished(0, wait=False)
            split(LEAD + 2)
            split(LEAD + 3)
            finished(1, wait=False)
            dve.wait_ge(root_made, roots.add())
            nc.vector.reciprocal(head_r[:], head_r[:]).then_inc(rstd_made, 1)
            with loop(4, 2, [0, 1], {bcasts: 4, highs: 4}) as i:
                for c in range(2):
                    for b in range(2):
                        h = 2 * c + b
                        split(2 * c + b + LEAD)
                        dve.wait_ge(head_bcast, bcasts.add())
                        nc.vector.tensor_tensor(scaled[h % 2][:], bcast_ps[h % 2][:, 0:T], flat(head_o, 4 * i + h),
                                                ALU.mult).then_inc(head_scaled, 1)
                        dve.wait_ge(heads_high, highs.add())
                        nc.vector.tensor_tensor(flat(heads_l, 4 * i + h), scaled[h % 2][:],
                                                flat(heads_h, 4 * i + h).bitcast(F32), ALU.subtract
                                                ).then_inc(heads_ready, 1)
                    finished(c, wait=False)
            for c in range(2):
                split(2 * c + LEAD)
                split(2 * c + LEAD + 1)
                finished(c, wait=False)

            with loop(KT // 2, 2, [0, 1], {steps: 4}) as i:
                for c in range(2):
                    split(2 * c + LEAD)
                    split(2 * c + LEAD + 1)
                    v = finished(c)
                    j = 2 * i + c
                    nc.vector.tensor_tensor(blend[:], acc[c][:, 0:T], flat(gate_a, j), ALU.mult).then_inc(acc_read[c], 1)
                    dve.wait_ge(acc_read[c], v)
                    dve.wait_ge(vec_step, step(nc.vector.tensor_tensor(blend2[:], blend[:], flat(conv_part, j), ALU.add)))
                    dve.wait_ge(vec_step, step(nc.vector.tensor_copy(flat(mixed_h, j), blend2[:])))
                    nc.vector.tensor_tensor(flat(mixed_l, j), blend2[:], flat(mixed_h, j).bitcast(F32),
                                            ALU.subtract).then_inc(mixed_ready, 1)

            def add_square(slot):
                dve.wait_ge(squares_made, squares.add())
                nc.vector.tensor_tensor(square_sum[:], square_sum[:], square[slot][:], ALU.add).then_inc(squares_read, 1)

            squares.add(KT)
            sq_read = Tally(2 + KT)
            with loop(KT // 2, 2, [0, 1], {squares: 2, sq_read: 2}):
                for c in range(2):
                    split(2 * c + LEAD)
                    split(2 * c + LEAD + 1)
                    finished(c, wait=False)
                    dve.wait_ge(squares_read, sq_read.value())
                    add_square(c)
                    sq_read.add()

            def add_normed(dst, src, gain, signal, signalled):
                with repeat(dve, KT // 2, {steps: 2, signalled: 2}) as i:
                    for c in range(2):
                        v = step(nc.vector.scalar_tensor_tensor(scaled[c][:], flat(src, 2 * i + c),
                                                                par[:, at(2 * i + (gain + c))], rstd[:],
                                                                ALU.mult, ALU.mult))
                    dve.wait_ge(vec_step, v)
                    for c in range(2):
                        nc.vector.tensor_tensor(flat(dst, 2 * i + c), flat(x, 2 * i + c), scaled[c][:],
                                                ALU.add).then_inc(signal, 1)
                    dve.wait_ge(signal, signalled.add(2))

            reciprocal_root()
            dve.wait_ge(rstd_made, 3)
            add_normed(x, mix_out, P_MIX_POST, resid_made, Tally())
            dve.wait_ge(vec_step, step(nc.vector.memset(square_sum[:], 0.0)))
            squares.add(KT)
            sq_read.add(KT)
            dve.wait_ge(resid_made, KT)
            reciprocal_root()
            dve.wait_ge(rstd_made, 4)
            norm(P_FFN_PRE)

            used = Tally(1)
            with loop(FT, 2, [0, 1], {steps: 3, taps: 2, silus: 1, used: 1}) as j:
                for c, dst in enumerate((up_a, up_b)):
                    split(2 * c + LEAD)
                    split(2 * c + LEAD + 1)
                    v = finished(c, wait=False)
                    dve.wait_ge(tap_ready, taps.add())
                    dve.wait_ge(vec_step, step(nc.vector.scalar_tensor_tensor(
                        dst[:, 1:T], acc[c][:, 0:T - 1], par[:, at(j + (P_UPCONV + 2 * FT + c * FT))], dst[:, 1:T],
                        ALU.mult, ALU.add)))
                    nc.vector.scalar_tensor_tensor(
                        dst[:, 2:T], acc[c][:, 0:T - 2], par[:, at(j + (P_UPCONV + c * FT))], dst[:, 2:T],
                        ALU.mult, ALU.add).then_inc(acc_read[c], 1)
                dve.wait_ge(acc_read[1], v)
                dve.wait_ge(silu_ready, silus.add())
                nc.vector.tensor_tensor(hidden[:], silu_a[:], up_b[:], ALU.mult).then_inc(hidden_read, 1)
                dve.wait_ge(hidden_read, used.add())
                dve.wait_ge(vec_step, step(nc.vector.tensor_copy(flat(hid_h, j), hidden[:])))
                nc.vector.tensor_tensor(flat(hid_l, j), hidden[:], flat(hid_h, j).bitcast(F32),
                                        ALU.subtract).then_inc(hidden_ready, 1)

            def down_pair(last):
                for c in range(2):
                    for n in range(DOWN_SLABS):
                        m = c * DOWN_SLABS + n + LEAD
                        if not last or m < 2 * DOWN_SLABS:
                            split(m, DOWN_SIZES[m % DOWN_SLABS])
                    finished(c, DOWN_SLABS, wait=False)
                    dve.wait_ge(squares_read, sq_read.value())
                    add_square(c)
                    sq_read.add()
            with repeat(dve, KT // 2 - 1, {slabs: 2 * DOWN_SLABS, cols: 2 * DOWN_SLABS, reads[0]: 1, reads[1]: 1,
                                           squares: 2, sq_read: 2}):
                down_pair(False)
            down_pair(True)
            reciprocal_root()
            dve.wait_ge(rstd_made, 5)
            add_normed(down_out, down_out, P_FFN_POST, out_made, Tally())

        @block.tensor
        def _(pe):
            slabs = Tally(RING)
            reads = [Tally() for _ in range(4)]
            squares, merged, qruns, vreads, osq, diags = (Tally() for _ in range(6))
            scaled_heads = Tally(HEADS)

            def slab(n, out, rhs_h, rhs_l, k0, size, last_k):
                s = n % RING
                pe.wait_ge(low_ready, slabs.add())
                for b in range(size):
                    k = k0 + b
                    nc.tensor.matmul(out, high[s][:, b, :], rhs_h[:, k, :], start=(k == 0), stop=False)
                    nc.tensor.matmul(out, high[s][:, b, :], rhs_l[:, k, :], start=False, stop=False)
                    done = nc.tensor.matmul(out, low[s][:, b, :], rhs_h[:, k, :], start=False, stop=(k == last_k))
                done.then_inc(slabs_used, 1)

            def col(n, slot, rhs, ready=None, extra=None):
                pe.wait_ge(acc_read[slot], reads[slot].add())
                for b in range(2):
                    if ready:
                        pe.wait_ge(ready[0], ready[1] + (b + 1) * SLAB)
                    slab(n + b, acc[slot][:, 0:T], rhs[0], rhs[1], b * SLAB, SLAB, KT - 1)
                    if extra:
                        extra(b)

            def loop(trips, n_cols, slots, more=None):
                per = {slabs: 2 * n_cols}
                for s in range(4):
                    per[reads[s]] = slots.count(s)
                per.update(more or {})
                return repeat(pe, trips, per)

            def channel_sum(src, out, start=True, stop=True):
                return nc.tensor.matmul(out, ones[:], src, start=start, stop=stop)

            pe.sem_inc(slabs_used, RING)
            pe.wait_ge(consts_made, 1)
            for k in range(KT):
                pe.wait_ge(squares_made, squares.add())
                done = channel_sum(square[k % 2][:], stat_ps[:, 0:T], k == 0, k == KT - 1)
                done.then_inc(squares_read if k < KT - 1 else sums_made, 1)
            pe.sem_inc(squares_read, 1)

            norm_hl, conv_hl, heads_hl = (norm_h, norm_l), (conv_h, conv_l), (heads_h, heads_l)
            mixed_hl, hid_hl = (mixed_h, mixed_l), (hid_h, hid_l)

            with loop(KT // 2, 6, [0, 1, 2] * 2):
                for c in range(6):
                    col(2 * c, c % 3, norm_hl, (normed, 0))
            with loop(KT, 2, [0, 1]):
                col(0, 0, norm_hl)
                col(2, 1, conv_hl, (conv_ready, 0))

            def score_level(s):
                if s == LEVELS:
                    done = nc.tensor.matmul(level_ps[:, 0:CHUNK], k_run[:, 0:CHUNK], q_run[:, CHUNK:T],
                                            start=True, stop=True)
                else:
                    h = 1 << s
                    keys = key if s == 0 else k_run
                    q = q_run[:].rearrange("p (c b u h) -> p c b u h", c=2, u=2, h=h)
                    for c in range(2):
                        done = nc.tensor.matmul(
                            level_ps[:, c * 64:c * 64 + 64].rearrange("p (b h) -> p b h", h=h),
                            keys[:, c * CHUNK:(c + 1) * CHUNK], q[:, c, :, 1, :], start=True, stop=True)
                done.then_inc(level_scored, 1)

            def head_extras(b, c, levels_on, out_on, head):
                s = 2 * c + b
                if s == 0 and out_on:
                    pe.wait_ge(level_merged, merged.add())
                    pe.wait_ge(v_ready, vreads.add())
                    nc.tensor.matmul(o_ps[:, 0:T], v_tok[:, 0, :], scores[:, 0:2, :].rearrange("p a t -> p (a t)"), start=True, stop=False)
                    nc.tensor.matmul(o_ps[:, CHUNK:T], v_tok[:, 1, :], scores[:, 2, :], start=False, stop=True
                                     ).then_inc(o_made, 1)
                if s == 0 and levels_on:
                    pe.wait_ge(q_run_ready, qruns.add())
                    for c2 in range(2):
                        t = slice(c2 * CHUNK, (c2 + 1) * CHUNK)
                        nc.tensor.matmul(level_ps[:, CHUNK + c2 * CHUNK:2 * CHUNK + c2 * CHUNK], key[:, t], query[:, t],
                                         start=True, stop=True)
                    score_level(0)
                if s == 1 and levels_on:
                    pe.wait_ge(acc_read[2], reads[2].value())
                    for c2 in range(2):
                        done = nc.tensor.transpose(v_ps[:, c2 * P:(c2 + 1) * P], v_chan[:, c2 * P:(c2 + 1) * P], ident[:])
                    done.then_inc(v_transposed, 1)
                if s > 0 and levels_on:
                    pe.wait_ge(level_merged, merged.add())
                    score_level(s)
                if s == 2 and out_on:
                    pe.wait_ge(o_squared, osq.add())
                    for half in range(2):
                        done = nc.tensor.matmul(stat_ps[:, at(head + half * HEADS)],
                                                o_square[:, half * P:(half + 1) * P], ones[:, 0:1],
                                                start=True, stop=True)
                    done.then_inc(head_summed, 1)

            def head(levels_on, out_on, i):
                for c in range(4):
                    col(2 * c, c, norm_hl, None, lambda b, c=c: head_extras(b, c, levels_on, out_on, i))

            head(False, False, None)
            head(True, False, None)
            with loop(HEADS - 2, 4, [0, 1, 2, 3], {merged: LEVELS + 1, qruns: 1, vreads: 1, osq: 1}) as i:
                head(True, True, i)
            head(True, True, HEADS - 2)
            for c in range(2):
                col(2 * c, c, norm_hl, None, lambda b, c=c: head_extras(b, c, False, True, HEADS - 1))
            with loop(4, 2, [0, 1], {diags: 4, scaled_heads: 4}):
                for c in range(2):
                    def spread(b, c=c):
                        h = 2 * c + b
                        pe.wait_ge(diag_ready, diags.add())
                        pe.wait_ge(head_scaled, scaled_heads.value() - 1)
                        scaled_heads.add()
                        nc.tensor.matmul(bcast_ps[h % 2][:, 0:T], ones[:], diag[h % 2][:].rearrange("p a b -> p (a b)"),
                                         start=True, stop=True).then_inc(head_bcast, 1)
                    col(2 * c, c, norm_hl, None, spread)
            for c in range(2):
                col(2 * c, c, norm_hl)
            with loop(KT // 2, 2, [0, 1]):
                for c in range(2):
                    col(2 * c, c, heads_hl, (heads_ready, 0))
            with loop(KT // 2, 2, [0, 1]):
                for c in range(2):
                    col(2 * c, c, mixed_hl, (mixed_ready, 0))
            pe.wait_ge(squares_read, 2 + 2 * KT)
            channel_sum(square_sum[:], stat_ps[:, 0:T]).then_inc(sums_made, 1)
            squares.add(KT)
            pe.wait_ge(root_made, 3)
            for k in range(KT):
                pe.wait_ge(squares_made, squares.add())
                done = channel_sum(square[k % 2][:], stat_ps[:, 0:T], k == 0, k == KT - 1)
                done.then_inc(squares_read if k < KT - 1 else sums_made, 1)
            pe.sem_inc(squares_read, 1)
            with loop(FT, 2, [0, 1]):
                for c in range(2):
                    col(2 * c, c, norm_hl, (normed, KT))
            with repeat(pe, KT // 2, {slabs: 2 * DOWN_SLABS, reads[0]: 1, reads[1]: 1}):
                for c in range(2):
                    pe.wait_ge(acc_read[c], reads[c].add())
                    for n in range(DOWN_SLABS):
                        if n in (0, DOWN_SLABS - 1):
                            pe.wait_ge(hidden_ready, SLAB * (DOWN_SLABS - 1) if n == 0 else FT)
                        slab(c * DOWN_SLABS + n, acc[c][:, 0:T], hid_hl[0], hid_hl[1], n * SLAB, DOWN_SIZES[n], FT - 1)
            pe.wait_ge(squares_read, 2 + 4 * KT)
            channel_sum(square_sum[:], stat_ps[:, 0:T]).then_inc(sums_made, 1)


def kernel(**inputs):
    import concourse.bacc as bacc
    from concourse.bass_utils import run_bass_kernel_spmd

    a = {k: np.asarray(v) for k, v in inputs.items()}

    def slabs(w):
        n = w.shape[1] // P
        return w.reshape(KT // SLAB, SLAB, P, n, P).transpose(3, 0, 2, 1, 4)

    names = ("q", "f", "i", "g", "cb", "cc", "ch", "ga", "gb")
    w_in = slabs(a["w_in"][0])
    w = {name: w_in[n * KT:(n + 1) * KT] for n, name in enumerate(names)}
    w["sc_out"], w["hg_out"], w["mix"] = (slabs(a[n][0]) for n in ("w_sc_out", "w_hg_out", "w_mix_out"))
    up = slabs(a["w_ffn_up"][0])
    w["up_a"], w["up_b"] = up[:FT], up[FT:]
    w_main = np.empty((COLS_MAIN, KT // SLAB, P, SLAB, P), np.float32)
    start = 0
    for group in (("cc", "ch", "cb"), ("gb", "sc_out"), ("f", "q", "i", "g"), ("ga",), ("hg_out",), ("mix",),
                  ("up_a", "up_b")):
        n = len(w[group[0]])
        for m, name in enumerate(group):
            w_main[start + m:start + n * len(group):len(group)] = w[name]
        start += n * len(group)
    w_main = w_main.reshape(SLABS_MAIN, P, SLAB, P)
    w_down = np.ascontiguousarray(a["w_ffn_down"][0].reshape(FT, P, KT, P).transpose(2, 1, 0, 3))

    def channels(v):
        return v.reshape(-1, P).T

    params = np.ascontiguousarray(np.concatenate([channels(v) for v in (
        a["norm_mix_pre"][0], a["norm_mix_post"][0], a["norm_ffn_pre"][0], a["norm_ffn_post"][0],
        a["hg_lower_bounds"][0], a["hg_out_norm"][0], a["sc_conv"][0], a["ffn_conv"][0], a["ffn_conv_bias"][0])], axis=1))

    def tiles(v):
        return np.ascontiguousarray(v.T.reshape(KT, P, T).transpose(1, 0, 2))

    ident = np.eye(P, dtype=np.float32)
    masks = np.zeros((P, LEVELS, 2, CHUNK // 2), np.float32)
    for lv in range(LEVELS):
        h = 1 << lv
        for s in range(P):
            if s % (2 * h) < h:
                b = s // (2 * h)
                masks[s, lv, :, b * h:(b + 1) * h] = 1

    nc = bacc.Bacc("TRN2", target_bir_lowering=False, num_devices=1)
    arrays = {"xT": tiles(a["x"][0]), "params": params, "ident_c": ident, "masks_c": masks,
              "w_main": w_main, "w_down": w_down}
    aps = [nc.dram_tensor(n, list(v.shape), mybir.dt.from_np(v.dtype), kind="ExternalInput").ap() for n, v in arrays.items()]
    out = nc.dram_tensor("outT", [P, KT, T], F32, kind="ExternalOutput").ap()
    build(nc, *aps, out)
    r = run_bass_kernel_spmd(nc, [arrays], core_ids=[0])
    y = np.asarray(r.results[0]["outT"])
    return np.ascontiguousarray(y.transpose(2, 1, 0).reshape(1, T, D_MODEL))
```

```python
from contextlib import ExitStack, contextmanager

import numpy as np

import concourse.bass as bass
from concourse import mybir

P = 128
D_MODEL = 2048
T = 256
HEADS = 16
FFN = 5632
KT = D_MODEL // P
FT = FFN // P
CHUNK = 128
LEVELS = 7
QUARTER = KT // 4
EPS = 1e-6
F_MIN = 1e-30

SLAB = 8
RING = 4
LEAD = 3
COLS_MAIN = 9 * KT + 3 * KT + 2 * FT
SLABS_MAIN = COLS_MAIN * KT // SLAB
DOWN_SIZES = [SLAB] * (FT // SLAB) + [FT % SLAB]
DOWN_SLABS = len(DOWN_SIZES)

P_MIX_PRE, P_MIX_POST, P_FFN_PRE, P_FFN_POST, P_LOWER = (KT * n for n in range(5))
P_HEAD_NORM = 5 * KT
P_CONV = P_HEAD_NORM + 1
P_UPCONV = P_CONV + 3 * KT
P_UPBIAS = P_UPCONV + 3 * 2 * FT
N_PARAMS = P_UPBIAS + 2 * FT

F32 = mybir.dt.float32
F32R = mybir.dt.float32r
U8 = mybir.dt.uint8
ACT = mybir.ActivationFunctionType
ALU = mybir.AluOpType


class Tally:

    def __init__(self, n=0):
        self.n, self.trip = n, 0

    def add(self, k=1):
        self.n += k
        return self.value()

    def value(self):
        return self.trip + self.n


@contextmanager
def repeat(eng, trips, per_trip):
    before = {t: t.n for t in per_trip}
    with eng.Fori(0, trips) as i:
        for t, k in per_trip.items():
            t.trip = i * k
        yield i
    for t, k in per_trip.items():
        assert t.n - before[t] == k, (t.n - before[t], k)
        t.trip = 0
        t.n += k * (trips - 1)


def at(i, c=1):
    return bass.ds(i, c)


def build(nc, xT, params, ident_d, masks_d, w_main, w_down, outT):
    ctx = ExitStack()
    with ctx:
        BASE = 16512
        KB = 1024

        def sb(name, shape, dt, off):
            return nc.alloc_sbuf_tensor_at(name, [P] + shape, dt, offset=BASE + off)

        tile_b = T * 4
        act_b = KT * tile_b
        gained_h = sb("gained_h", [KT, T], F32R, 0)
        gained_l = sb("gained_l", [KT, T], F32R, act_b)
        down_out = sb("down_out", [KT, T], F32, 0)
        squares = sb("squares", [4, QUARTER * T], F32, 48 * KB)
        gained = sb("gained", [KT, T], F32, 112 * KB)
        conv_h = sb("conv_h", [KT, T], F32R, 32 * KB)
        conv_l = sb("conv_l", [KT, T], F32R, 48 * KB)
        heads_h = sb("heads_h", [KT, T], F32R, 32 * KB)
        heads_l = sb("heads_l", [KT, T], F32R, 48 * KB)
        mix_out = sb("mix_out", [KT, T], F32, 32 * KB)
        head_o = sb("head_o", [HEADS, T], F32, 64 * KB)
        masks_f = sb("masks_f", [LEVELS, CHUNK // 2], F32, 64 * KB)
        head_g = sb("head_g", [HEADS, T], F32, 80 * KB)
        mixed_h = sb("mixed_h", [KT, T], F32R, 64 * KB)
        mixed_l = sb("mixed_l", [KT, T], F32R, 80 * KB)
        conv_part = sb("conv_part", [KT, T], F32, 96 * KB)
        gate_a = sb("gate_a", [KT, T], F32, 112 * KB)
        hid_h = sb("hid_h", [FT, T], F32R, 32 * KB)
        hid_l = sb("hid_l", [FT, T], F32R, 76 * KB)
        x = sb("x", [KT, T], F32, 128 * KB)
        raw = [sb(f"raw{s}", [SLAB, P], F32, (144 + 4 * s) * KB) for s in range(RING)]
        high = [sb(f"high{s}", [SLAB, P], F32R, (160 + 4 * s) * KB) for s in range(RING)]
        low = [sb(f"low{s}", [SLAB, P], F32R, (176 + 4 * s) * KB) for s in range(RING)]
        off = 192 * KB
        par = sb("par", [N_PARAMS], F32, off); off += -(-N_PARAMS * 4 // 32) * 32
        ident = sb("ident", [P], F32, off); off += P * 4
        ones = sb("ones", [P], F32, off); off += P * 4
        masks = sb("masks", [LEVELS, 2, CHUNK // 2], U8, off); off += LEVELS * CHUNK
        eps = sb("eps", [1], F32, off); off += 32
        lower = sb("lower", [KT], F32, off); off += KT * 4
        upper = sb("upper", [KT], F32, off); off += KT * 4
        neg_upper = sb("neg_upper", [KT], F32, off); off += KT * 4
        warm = sb("warm", [1], F32, off); off += 32
        head_r = sb("head_r", [2, HEADS], F32, off); off += 2 * HEADS * 4
        G = off
        slot = tile_b + 32
        assert BASE + G + 10 * slot <= 229344, BASE + G + 10 * slot

        def work(name, n, dt=F32, cols=T):
            return sb(name, [cols], dt, G + n * slot)

        ch_cc = work("ch_cc", 0, cols=T + 2)
        cc = work("cc", 1)
        conv_u = work("conv_u", 2)
        conv_y = work("conv_y", 3)
        gate_b = work("gate_b", 4)
        gate_in = [work("gate_in0", 7), work("gate_in1", 6)]
        rstd2 = work("rstd2", 5)
        square = [work("square0", 5), work("square1", 6)]
        square_sum = work("square_sum", 7)
        root = work("root", 8)
        rstd = work("rstd", 9)
        scaled = [work("scaled0", 3), work("scaled1", 4)]
        diag = [sb(f"diag{n}", [2, P], F32, G + n * slot) for n in range(2)]
        blend = work("blend", 2)
        blend2 = work("blend2", 3)
        up_raw = [work("up_raw0", 4), work("up_raw1", 5)]
        up_a = work("up_a", 0)
        up_b = work("up_b", 1)
        silu_a = work("silu_a", 2)
        hidden = work("hidden", 3)

        R = 32 * KB
        def rec(name, n, shape):
            return sb(name, shape, F32, R + n * KB)
        f_sig = rec("f_sig", 0, [T])
        f_gate = rec("f_gate", 1, [T])
        key = rec("key", 2, [T])
        q_sig = rec("q_sig", 3, [T])
        query = rec("query", 4, [T])
        q_run = rec("q_run", 5, [T])
        k_run = rec("k_run", 6, [T])
        v_chan = rec("v_chan", 7, [T])
        g_sig = rec("g_sig", 8, [T])
        totals = rec("totals", 9, [T])
        v_tok = rec("v_tok", 10, [2, P])
        o_square = rec("o_square", 11, [T])
        f_in = rec("f_in", 14, [T])
        q_in = rec("q_in", 15, [T])
        g_in = rec("g_in", 16, [T])
        scores = rec("scores", 12, [3, CHUNK])

        acc = [nc.alloc_psum_tensor(f"acc{n}", [P, 512], F32) for n in range(4)]
        level_ps = nc.alloc_psum_tensor("level_ps", [P, 512], F32)
        o_ps = nc.alloc_psum_tensor("o_ps", [P, 512], F32)
        v_ps = nc.alloc_psum_tensor("v_ps", [P, 512], F32)
        stat_ps = nc.alloc_psum_tensor("stat_ps", [P, 512], F32)
        bcast_ps = [level_ps, o_ps]

        def sem(name):
            return nc.alloc_semaphore(name)

        x_loaded = [sem(f"x_loaded{n}") for n in range(4)]
        params_loaded = sem("params_loaded")
        consts_loaded = sem("consts_loaded")
        raw_loaded = [sem(f"raw_loaded{s}") for s in range(RING)]
        high_ready = sem("high_ready")
        low_ready = sem("low_ready")
        slabs_used = sem("slabs_used")
        acc_read = [sem(f"acc_read{n}") for n in range(4)]
        vec_step = sem("vec_step")
        bound_shifted = sem("bound_shifted")
        bound_exp = sem("bound_exp")
        consts_made = sem("consts_made")
        squares_made = sem("squares_made")
        squares_read = sem("squares_read")
        quarters_squared = sem("quarters_squared")
        gained_made = sem("gained_made")
        gained_high = sem("gained_high")
        gained_ready = sem("gained_ready")
        square_sum_made = sem("square_sum_made")
        sums_made = sem("sums_made")
        root_made = sem("root_made")
        rstd_made = sem("rstd_made")
        resid_made = sem("resid_made")
        conv_ready = sem("conv_ready")
        gate_ready = sem("gate_ready")
        key_ready = sem("key_ready")
        f_sig_ready = sem("f_sig_ready")
        q_sig_ready = sem("q_sig_ready")
        g_sig_ready = sem("g_sig_ready")
        k_run_ready = sem("k_run_ready")
        q_run_ready = sem("q_run_ready")
        level_scored = sem("level_scored")
        level_merged = sem("level_merged")
        v_transposed = sem("v_transposed")
        v_ready = sem("v_ready")
        o_made = sem("o_made")
        o_squared = sem("o_squared")
        head_summed = sem("head_summed")
        diag_ready = sem("diag_ready")
        head_bcast = sem("head_bcast")
        head_scaled = sem("head_scaled")
        heads_high = sem("heads_high")
        heads_ready = sem("heads_ready")
        mixed_ready = sem("mixed_ready")
        taps_made = sem("taps_made")
        tap_ready = sem("tap_ready")
        silu_ready = sem("silu_ready")
        hidden_read = sem("hidden_read")
        hidden_ready = sem("hidden_ready")
        out_made = sem("out_made")
        stored = sem("stored")

        block = ctx.enter_context(nc.Block())

        @block.sync
        def _(sp):
            def quarter(n):
                t = slice(n * QUARTER, (n + 1) * QUARTER)
                sp.dma_start(x[:, t, :], xT[:, t, :]).then_inc(x_loaded[n], 16)

            def first_slab(s):
                sp.dma_start(raw[s][:], w_main[s]).then_inc(raw_loaded[s], 16)

            sp.dma_start(par[:], params).then_inc(params_loaded, 16)
            for n in range(4):
                quarter(n)
                first_slab(n)
            sp.dma_start(ident[:], ident_d).then_inc(consts_loaded, 16)
            sp.dma_start(masks_f[:], masks_d).then_inc(consts_loaded, 16)
            freed = Tally(RING)
            with repeat(sp, SLABS_MAIN // RING - 1, {freed: RING}) as i:
                for s in range(RING):
                    sp.wait_ge(low_ready, freed.add())
                    sp.dma_start(raw[s][:], w_main[at((i + 1) * RING + s), :, :, :].rearrange("o p k c -> p (o k) c")
                                 ).then_inc(raw_loaded[s], 16)
            with repeat(sp, KT // 2, {freed: 2 * DOWN_SLABS}) as i:
                for m in range(2 * DOWN_SLABS):
                    n = m % DOWN_SLABS
                    sp.wait_ge(low_ready, freed.add())
                    sp.dma_start(raw[m % RING][:, 0:DOWN_SIZES[n], :],
                                 w_down[at(2 * i + m // DOWN_SLABS), :, n * SLAB:n * SLAB + DOWN_SIZES[n], :]
                                 .rearrange("o p k c -> p (o k) c")).then_inc(raw_loaded[m % RING], 16)
            for n in range(4):
                sp.wait_ge(out_made, n + 1)
                t = slice(n * QUARTER, (n + 1) * QUARTER)
                sp.dma_start(outT[:, t, :], down_out[:, t, :]).then_inc(stored, 16)
            sp.wait_ge(stored, 64)

        @block.scalar
        def _(act):
            slabs = Tally()
            loads = [Tally() for _ in range(RING)]
            cols = Tally(RING)
            reads = [Tally(1) for _ in range(4)]
            squares_out = Tally(2)
            keys, sums, levels, outs, vts, gained_q, resid = (Tally() for _ in range(7))

            def split(n, size=SLAB):
                s = n % RING
                act.wait_ge(raw_loaded[s], loads[s].add(16))
                act.wait_ge(slabs_used, slabs.add())
                nc.scalar.activation(high[s][:, 0:size, :], raw[s][:, 0:size, :], ACT.Copy).then_inc(high_ready, 1)

            def finished(slot, n=2, wait=True):
                v = cols.add(n)
                if wait:
                    act.wait_ge(slabs_used, v)
                reads[slot].add()

            def scaled_in(slot):
                cols.add(2)
                act.wait_ge(acc_read[slot], reads[slot].add())

            def quarter(t, q):
                return t[:, q * QUARTER:(q + 1) * QUARTER, :].rearrange("p a t -> p (a t)")

            def gained_parts(q):
                act.wait_ge(gained_made, gained_q.add())
                nc.scalar.activation(quarter(gained_h, q), quarter(gained, q), ACT.Copy).then_inc(gained_high, 1)

            def quarter_squares(q):
                nc.scalar.activation(squares[:, q, :], quarter(x, q), ACT.Square).then_inc(quarters_squared, 1)

            def loop(trips, n_cols, slots, more=None):
                n = 2 * n_cols
                per = {slabs: n, cols: n}
                for s in range(RING):
                    per[loads[s]] = 16 * n // RING
                for s in range(4):
                    per[reads[s]] = slots.count(s)
                per.update(more or {})
                return repeat(act, trips, per)

            def root_of(ps, out, scale):
                act.wait_ge(sums_made, sums.add())
                nc.scalar.activation(out, ps, ACT.Sqrt, bias=eps[:], scale=scale).then_inc(root_made, 1)

            act.wait_ge(consts_made, 2)
            nc.scalar.activation(warm[:], eps[:], ACT.Sqrt)
            for q in range(4):
                gained_parts(q)
                if q < LEAD:
                    split(q)
                quarter_squares(q)

            def conv_pair(first):
                for c in range(6):
                    split(2 * c + LEAD)
                    if first and c == 1:
                        root_of(stat_ps[:, 0:T], root[:], 1.0 / D_MODEL)
                    split(2 * c + LEAD + 1)
                    finished(c % 3, wait=c % 3 == 0)
                    if c % 3 == 0:
                        act.wait_ge(acc_read[1], reads[1].value())
                        nc.scalar.activation(cc[:], acc[0][:, 0:T], ACT.Copy).then_inc(acc_read[0], 1)
                if first:
                    act.wait_ge(bound_shifted, 1)
                    nc.scalar.activation(neg_upper[:], lower[:], ACT.Exp).then_inc(bound_exp, 1)

            conv_pair(True)
            with loop(KT // 2 - 1, 6, [0, 1, 2] * 2):
                conv_pair(False)

            with loop(KT, 2, [0, 1]) as j:
                split(LEAD)
                split(LEAD + 1)
                scaled_in(0)
                nc.scalar.activation(gate_b[:], gate_in[0][:], ACT.Sigmoid).then_inc(gate_ready, 1)
                split(LEAD + 2)
                split(LEAD + 3)
                finished(1, wait=False)

            def head_extra_a(out_on):
                if out_on:
                    act.wait_ge(o_made, outs.add())
                    nc.scalar.activation(o_square[:], o_ps[:, 0:T], ACT.Square).then_inc(o_squared, 1)

            def head_extra_b(levels_on):
                if levels_on:
                    act.wait_ge(v_transposed, vts.add())
                    nc.scalar.activation(v_tok[:], v_ps[:, 0:T].rearrange("p (a b) -> p a b", a=2),
                                         ACT.Copy).then_inc(v_ready, 1)

            def head(levels_on, out_on):
                split(LEAD)
                head_extra_a(out_on)
                split(LEAD + 1)
                head_extra_b(levels_on)
                scaled_in(0)
                nc.scalar.activation(f_sig[:], f_in[:], ACT.Sigmoid).then_inc(f_sig_ready, 1)
                split(LEAD + 2)
                split(LEAD + 3)
                scaled_in(1)
                nc.scalar.activation(q_sig[:], q_in[:], ACT.Sigmoid).then_inc(q_sig_ready, 1)
                split(LEAD + 4)
                split(LEAD + 5)
                scaled_in(2)
                nc.scalar.activation(g_sig[:], g_in[:], ACT.Sigmoid).then_inc(g_sig_ready, 1)
                split(LEAD + 6)
                split(LEAD + 7)
                finished(3, wait=False)
                act.wait_ge(key_ready, keys.add())
                if levels_on:
                    act.wait_ge(level_scored, levels.add(LEVELS + 1))
                nc.scalar.activation(k_run[:], key[:], ACT.Copy).then_inc(k_run_ready, 1)

            head(False, False)
            head(True, False)
            with loop(HEADS - 2, 4, [0, 1, 2, 3], {keys: 1, levels: LEVELS + 1, outs: 1, vts: 1}):
                head(True, True)

            def gate_tile(slot, j):
                scaled_in(slot)
                nc.scalar.activation(gate_a[:, at(j), :].rearrange("p a t -> p (a t)"), gate_in[slot % 2][:],
                                     ACT.Sigmoid).then_inc(gate_ready, 1)

            for c in range(4):
                split(2 * c + LEAD)
                if c == 0:
                    head_extra_a(True)
                split(2 * c + LEAD + 1)
                if c == 0:
                    head_extra_b(True)
                gate_tile(c, c)
            split(LEAD)
            head_extra_a(True)
            split(LEAD + 1)
            gate_tile(0, 4)
            split(LEAD + 2)
            split(LEAD + 3)
            gate_tile(1, 5)
            act.wait_ge(head_summed, HEADS)
            nc.scalar.activation(head_r[:], stat_ps[:, 0:2 * HEADS].rearrange("p (a b) -> p a b", a=2),
                                 ACT.Sqrt, bias=eps[:], scale=1.0 / P).then_inc(root_made, 1)
            scaleds = Tally(HEADS)
            with loop(4, 2, [0, 1], {scaleds: 4}) as i:
                for c in range(2):
                    for b in range(2):
                        split(2 * c + b + LEAD)
                        h = 2 * c + b
                        if c == 0 and b == 0:
                            act.wait_ge(rstd_made, 2)
                        for half in range(2):
                            done = nc.scalar.activation(diag[h % 2][:, half, :], ident[:], ACT.Copy,
                                                        scale=head_r[:, half, at(4 * i + h)])
                        done.then_inc(diag_ready, 1)
                        act.wait_ge(head_scaled, scaleds.add())
                        nc.scalar.activation(heads_h[:, at(4 * i + h), :].rearrange("p a t -> p (a t)"),
                                             scaled[h % 2][:], ACT.Copy).then_inc(heads_high, 1)
                    gate_tile(c, 2 * i + 6 + c)
            for c in range(2):
                split(2 * c + LEAD)
                split(2 * c + LEAD + 1)
                gate_tile(c, 14 + c)

            with loop(KT // 2, 2, [0, 1]):
                for c in range(2):
                    split(2 * c + LEAD)
                    split(2 * c + LEAD + 1)
                    finished(c, wait=False)

            def out_tile(dst, slot, j, gain):
                act.wait_ge(squares_read, squares_out.value() - 1)
                squares_out.add()
                nc.scalar.activation(square[slot][:], acc[slot][:, 0:T], ACT.Square).then_inc(squares_made, 1)
                nc.scalar.activation(dst[:, at(j), :].rearrange("p a t -> p (a t)"), acc[slot][:, 0:T], ACT.Copy,
                                     scale=par[:, at(j + gain)]).then_inc(acc_read[slot], 1)

            nc.scalar.activation(warm[:], eps[:], ACT.Sqrt)
            with loop(KT // 2, 2, [0, 1], {squares_out: 2}) as i:
                for c in range(2):
                    split(2 * c + LEAD)
                    split(2 * c + LEAD + 1)
                    finished(c)
                    out_tile(mix_out, c, 2 * i + c, P_MIX_POST)
            root_of(stat_ps[:, 0:T], root[:], 1.0 / D_MODEL)
            for q in range(4):
                act.wait_ge(resid_made, resid.add())
                for k in range(q * QUARTER, (q + 1) * QUARTER):
                    done = nc.scalar.activation(gained[:, k, :], x[:, k, :], ACT.Copy,
                                                scale=par[:, P_FFN_PRE + k:P_FFN_PRE + k + 1])
                done.then_inc(gained_made, 1)
                gained_parts(q)
                quarter_squares(q)

            used = Tally(1)
            a_taps = Tally()

            def up_loop():
                return loop(FT - 1, 2, [0, 1], {used: 1, a_taps: 1})

            def tap(j, c, dst):
                scaled_in(c)
                if c == 0:
                    act.wait_ge(hidden_read, used.add() - 1)
                nc.scalar.activation(dst[:], up_raw[c][:], ACT.Identity, bias=par[:, at(j + (P_UPBIAS + c * FT))],
                                     scale=par[:, at(j + (P_UPCONV + 4 * FT + c * FT))]).then_inc(tap_ready, 1)

            def up_pair(j, first):
                split(LEAD)
                if not first:
                    tap(j - 1, 1, up_b)
                split(LEAD + 1)
                if first:
                    root_of(stat_ps[:, 0:T], root[:], 1.0 / D_MODEL)
                split(LEAD + 2)
                tap(j, 0, up_a)
                split(LEAD + 3)
                act.wait_ge(taps_made, a_taps.add())
                nc.scalar.activation(silu_a[:], up_a[:], ACT.Silu).then_inc(silu_ready, 1)

            up_pair(0, True)
            with up_loop() as j:
                up_pair(j + 1, False)

            per = {slabs: 2 * DOWN_SLABS, cols: 2 * DOWN_SLABS, reads[0]: 1, reads[1]: 1, squares_out: 2}
            for s in range(RING):
                per[loads[s]] = 16 * 2 * DOWN_SLABS // RING

            def down_pair(i, first, last):
                for c in range(2):
                    for n in range(DOWN_SLABS):
                        m = c * DOWN_SLABS + n + LEAD
                        if not last or m < 2 * DOWN_SLABS:
                            split(m, DOWN_SIZES[m % DOWN_SLABS])
                        if first and c == 0 and n == 0:
                            tap(FT - 1, 1, up_b)
                            nc.scalar.activation(warm[:], eps[:], ACT.Sqrt)
                    finished(c, DOWN_SLABS)
                    out_tile(down_out, c, 2 * i + c, P_FFN_POST)
            down_pair(0, True, False)
            with repeat(act, KT // 2 - 2, per) as i:
                down_pair(i + 1, False, False)
            down_pair(KT // 2 - 1, False, True)
            root_of(stat_ps[:, 0:T], root[:], 1.0 / D_MODEL)

        @block.vector
        def _(dve):
            slabs = Tally()
            cols = Tally(RING)
            reads = [Tally(1) for _ in range(4)]
            steps = Tally()
            (squares_in, roots, fs, qs, gs, krs, scored, outs, bcasts, highs, taps, silus, gates, gained_q, gained_l_made,
             quarter_sq, rstds) = (Tally() for _ in range(17))
            gate_outs = Tally(-1)

            def step(ins):
                ins.then_inc(vec_step, 1)
                return steps.add()

            def split(n, size=SLAB):
                s = n % RING
                dve.wait_ge(high_ready, slabs.add())
                nc.vector.tensor_tensor(low[s][:, 0:size, :], raw[s][:, 0:size, :], high[s][:, 0:size, :].bitcast(F32),
                                        ALU.subtract).then_inc(low_ready, 1)

            def finished(slot, n=2, wait=True):
                v = cols.add(n)
                if wait:
                    dve.wait_ge(slabs_used, v)
                return reads[slot].add()

            def loop(trips, n_cols, slots, more=None):
                per = {slabs: 2 * n_cols, cols: 2 * n_cols}
                for s in range(4):
                    per[reads[s]] = slots.count(s)
                per.update(more or {})
                return repeat(dve, trips, per)

            def flat(t, i):
                return t[:, at(i), :].rearrange("p a t -> p (a t)")

            def quarter(t, q):
                return t[:, q * QUARTER:(q + 1) * QUARTER, :].rearrange("p a t -> p (a t)")

            def over_quarter(t):
                return t[:].rearrange("p (o t) -> p o t", o=1).broadcast_to([P, QUARTER, T])

            def reciprocal_root():
                dve.wait_ge(root_made, roots.add())
                nc.vector.reciprocal(rstd[:], root[:]).then_inc(rstd_made, 1)
                dve.wait_ge(rstd_made, rstds.add())

            def times_gain(q, gain):
                for k in range(q * QUARTER, (q + 1) * QUARTER):
                    done = nc.vector.tensor_scalar(gained[:, k, :], x[:, k, :], par[:, gain + k:gain + k + 1], None, ALU.mult)
                done.then_inc(gained_made, 1)

            def gained_low(q):
                dve.wait_ge(gained_high, gained_q.add())
                nc.vector.tensor_tensor(quarter(gained_l, q), quarter(gained, q), quarter(gained_h, q).bitcast(F32),
                                        ALU.subtract).then_inc(gained_ready, 1)

            def add_quarter(q):
                dve.wait_ge(quarters_squared, quarter_sq.add())
                if q:
                    dve.wait_ge(vec_step, step(nc.vector.tensor_tensor(squares[:, 0, :], squares[:, 0, :], squares[:, q, :],
                                                                       ALU.add)))

            def fold_squares():
                half = QUARTER * T // 2
                dve.wait_ge(vec_step, step(nc.vector.tensor_tensor(squares[:, 0, 0:half], squares[:, 0, 0:half],
                                                                   squares[:, 0, half:2 * half], ALU.add)))
                nc.vector.tensor_tensor(square_sum[:], squares[:, 0, 0:T], squares[:, 0, T:2 * T], ALU.add
                                        ).then_inc(square_sum_made, 1)

            def scale_tokens(slot, dst):
                v = finished(slot)
                nc.vector.tensor_tensor(dst, acc[slot][:, 0:T], rstd[:], ALU.mult).then_inc(acc_read[slot], 1)
                return v

            dve.sem_inc(low_ready, RING)
            for s in range(4):
                dve.sem_inc(acc_read[s], 1)
            dve.sem_inc(squares_read, 2)
            dve.sem_inc(hidden_read, 1)
            nc.vector.memset(ones[:], 1.0).then_inc(consts_made, 1)
            nc.vector.memset(eps[:], EPS).then_inc(consts_made, 1)
            step(nc.vector.memset(ch_cc[:, 0:2], 0.0))
            dve.wait_ge(params_loaded, 16)
            for q in range(4):
                dve.wait_ge(x_loaded[q], 16)
                times_gain(q, P_MIX_PRE)
                if q:
                    gained_low(q - 1)
                    split(q - 1)
            gained_low(3)
            for q in range(4):
                add_quarter(q)
            fold_squares()
            lb = par[:, P_LOWER:P_LOWER + KT]
            nc.vector.tensor_tensor(lower[:], lb, lb, ALU.subtract).then_inc(bound_shifted, 1)

            def lower_bounds():
                dve.wait_ge(bound_exp, 1)
                dve.wait_ge(vec_step, step(nc.vector.reciprocal(upper[:], neg_upper[:])))
                dve.wait_ge(vec_step, step(nc.vector.tensor_tensor(neg_upper[:], neg_upper[:], upper[:], ALU.mult)))
                dve.wait_ge(vec_step, step(nc.vector.tensor_tensor(lower[:], neg_upper[:], neg_upper[:], ALU.subtract)))
                step(nc.vector.tensor_scalar(upper[:], lower[:], -1.0, 1.0, ALU.mult, ALU.add))
                dve.wait_ge(vec_step, step(nc.vector.tensor_scalar(neg_upper[:], lower[:], -1.0, None, ALU.add)))

            def conv_pair(i, first):
                for h in range(2):
                    j = 2 * i + h
                    base = 6 * h
                    split(base + LEAD)
                    split(base + LEAD + 1)
                    cc_read = finished(0, wait=False)
                    split(base + LEAD + 2)
                    split(base + LEAD + 3)
                    if first and h == 0:
                        reciprocal_root()
                        dve.wait_ge(vec_step, step(nc.vector.tensor_tensor(rstd2[:], rstd[:], rstd[:], ALU.mult)))
                    v = finished(1)
                    dve.wait_ge(acc_read[0], cc_read)
                    nc.vector.tensor_tensor(ch_cc[:, 2:T + 2], acc[1][:, 0:T], cc[:], ALU.mult).then_inc(acc_read[1], 1)
                    dve.wait_ge(acc_read[1], v)
                    dve.wait_ge(vec_step, step(nc.vector.tensor_tensor(ch_cc[:, 2:T + 2], ch_cc[:, 2:T + 2], rstd2[:],
                                                                       ALU.mult)))
                    tap = [par[:, at(j + (P_CONV + n * KT))] for n in range(3)]
                    dve.wait_ge(vec_step, step(nc.vector.tensor_scalar(conv_u[:], ch_cc[:, 2:T + 2], tap[2], None, ALU.mult)))
                    dve.wait_ge(vec_step, step(nc.vector.scalar_tensor_tensor(conv_u[:], ch_cc[:, 1:T + 1], tap[1],
                                                                              conv_u[:], ALU.mult, ALU.add)))
                    dve.wait_ge(vec_step, step(nc.vector.scalar_tensor_tensor(conv_u[:], ch_cc[:, 0:T], tap[0],
                                                                              conv_u[:], ALU.mult, ALU.add)))
                    step(nc.vector.tensor_tensor(conv_u[:], conv_u[:], rstd[:], ALU.mult))
                    split(base + LEAD + 4)
                    split(base + LEAD + 5)
                    v = finished(2)
                    dve.wait_ge(vec_step, steps.value())
                    nc.vector.tensor_tensor(conv_y[:], acc[2][:, 0:T], conv_u[:], ALU.mult).then_inc(acc_read[2], 1)
                    dve.wait_ge(acc_read[2], v)
                    dve.wait_ge(vec_step, step(nc.vector.tensor_copy(flat(conv_h, j), conv_y[:])))
                    nc.vector.tensor_tensor(flat(conv_l, j), conv_y[:], flat(conv_h, j).bitcast(F32),
                                            ALU.subtract).then_inc(conv_ready, 1)

            conv_pair(0, True)
            lower_bounds()
            dve.wait_ge(consts_loaded, 32)
            for c in range(2):
                dve.wait_ge(vec_step, step(nc.vector.tensor_copy(masks[:, :, c, :], masks_f[:])))
            with loop(KT // 2 - 1, 6, [0, 1, 2] * 2, {steps: 12}) as i:
                conv_pair(i + 1, False)

            with loop(KT, 2, [0, 1], {gates: 1}) as j:
                split(LEAD)
                split(LEAD + 1)
                scale_tokens(0, gate_in[0][:])
                split(LEAD + 2)
                split(LEAD + 3)
                finished(1)
                dve.wait_ge(gate_ready, gates.add())
                nc.vector.tensor_tensor(flat(conv_part, j), acc[1][:, 0:T], gate_b[:], ALU.mult).then_inc(acc_read[1], 1)

            def total(level):
                if level == 0:
                    return f_gate[:]
                start = T - 2 * (T >> level)
                return totals[:, start:start + (T >> level)]

            def halves(t, h):
                return t[:].rearrange("p (b u h) -> p b u h", u=2, h=h)

            def merge(s):
                dve.wait_ge(level_scored, scored.add())
                if s == LEVELS:
                    nc.vector.tensor_copy(scores[:, 1, :], level_ps[:, 0:CHUNK]).then_inc(level_merged, 1)
                    return
                h = 1 << s
                if s == 0:
                    dve.wait_ge(k_run_ready, krs.add())
                    v = step(nc.vector.tensor_tensor(
                        scores[:, 0:3:2, :], level_ps[:, CHUNK:3 * CHUNK].rearrange("p (c t) -> p c t", c=2),
                        ident[:].rearrange("p (o t) -> p o t", o=1).broadcast_to([P, 2, CHUNK]), ALU.mult))
                tot = total(s).rearrange("p (b u o) -> p b u o", u=2, o=1)
                nb = T // (2 * h)
                nc.vector.tensor_tensor(halves(q_run, h)[:, :, 1, :], halves(q_run, h)[:, :, 1, :],
                                        tot[:, :, 0, :].broadcast_to([P, nb, h]), ALU.mult)
                nc.vector.tensor_tensor(halves(k_run, h)[:, :, 0, :], halves(k_run, h)[:, :, 0, :],
                                        tot[:, :, 1, :].broadcast_to([P, nb, h]), ALU.mult)
                if s == 0:
                    dve.wait_ge(vec_step, v)
                if s < LEVELS - 1:
                    t2 = total(s).rearrange("p (b u) -> p b u", u=2)
                    nc.vector.tensor_tensor(total(s + 1), t2[:, :, 0], t2[:, :, 1], ALU.mult)
                nc.vector.copy_predicated(
                    scores[:, 0:3:2, :].rearrange("p c (b u h) -> p c b u h", u=2, h=h)[:, :, :, 1, :],
                    masks[:, s, :, :].rearrange("p c (b h) -> p c b h", h=h),
                    level_ps[:, 0:CHUNK].rearrange("p (c b h) -> p c b h", c=2, h=h)).then_inc(level_merged, 1)

            def head_output(i):
                dve.wait_ge(o_squared, outs.add())
                nc.vector.tensor_tensor(flat(head_o, i), o_ps[:, 0:T], flat(head_g, i), ALU.mult).then_inc(head_scaled, 1)

            def head(i, levels_on, out_on):
                split(LEAD)
                if out_on:
                    head_output(i - 2)
                if levels_on:
                    merge(0)
                split(LEAD + 1)
                if levels_on:
                    merge(1)
                scale_tokens(0, f_in[:])
                split(LEAD + 2)
                if levels_on:
                    merge(2)
                dve.wait_ge(f_sig_ready, fs.add())
                dve.wait_ge(vec_step, step(nc.vector.tensor_scalar(f_gate[:], f_sig[:], upper[:, at(i)], lower[:, at(i)],
                                                                   ALU.mult, ALU.add)))
                step(nc.vector.tensor_scalar(f_gate[:], f_gate[:], F_MIN, None, ALU.max))
                nc.vector.tensor_scalar(key[:], f_sig[:], -1.0, neg_upper[:, at(i)], ALU.add, ALU.mult).then_inc(key_ready, 1)
                split(LEAD + 3)
                if levels_on:
                    merge(3)
                scale_tokens(1, q_in[:])
                split(LEAD + 4)
                if levels_on:
                    merge(4)
                dve.wait_ge(q_sig_ready, qs.add())
                step(nc.vector.tensor_tensor(query[:], q_in[:], q_sig[:], ALU.mult))
                split(LEAD + 5)
                if levels_on:
                    merge(5)
                scale_tokens(2, g_in[:])
                split(LEAD + 6)
                if levels_on:
                    merge(6)
                dve.wait_ge(g_sig_ready, gs.add())
                step(nc.vector.scalar_tensor_tensor(flat(head_g, i), g_in[:], par[:, P_HEAD_NORM:P_HEAD_NORM + 1],
                                                    g_sig[:], ALU.mult, ALU.mult))
                split(LEAD + 7)
                if levels_on:
                    merge(7)
                scale_tokens(3, v_chan[:])
                dve.wait_ge(vec_step, steps.value())
                nc.vector.tensor_tensor(q_run[:], query[:], f_gate[:], ALU.mult).then_inc(q_run_ready, 1)

            head(0, False, False)
            head(1, True, False)
            with loop(HEADS - 2, 4, [0, 1, 2, 3],
                      {steps: 5, scored: LEVELS + 1, krs: 1, fs: 1, qs: 1, gs: 1, outs: 1}) as i:
                head(i + 2, True, True)

            def gate_tile(slot):
                dve.wait_ge(gate_ready, gate_outs.add())
                scale_tokens(slot, gate_in[slot % 2][:])

            gate_outs.add(KT - 1)
            for c in range(4):
                split(2 * c + LEAD)
                if c == 0:
                    head_output(HEADS - 2)
                merge(2 * c)
                split(2 * c + LEAD + 1)
                merge(2 * c + 1)
                gate_tile(c)
            split(LEAD)
            head_output(HEADS - 1)
            split(LEAD + 1)
            gate_tile(0)
            split(LEAD + 2)
            split(LEAD + 3)
            gate_tile(1)
            dve.wait_ge(root_made, roots.add())
            nc.vector.reciprocal(head_r[:], head_r[:]).then_inc(rstd_made, 1)
            rstds.add()
            def head_low(h):
                dve.wait_ge(heads_high, highs.add())
                nc.vector.tensor_tensor(flat(heads_l, h[0]), scaled[h[1]][:], flat(heads_h, h[0]).bitcast(F32),
                                        ALU.subtract).then_inc(heads_ready, 1)

            lows = Tally(1)
            dve.sem_inc(heads_ready, 2)
            with loop(4, 2, [0, 1], {bcasts: 4, highs: 4, gate_outs: 2, lows: 4}) as i:
                for c in range(2):
                    for b in range(2):
                        h = 2 * c + b
                        split(2 * c + b + LEAD)
                        dve.wait_ge(heads_ready, lows.value())
                        dve.wait_ge(head_bcast, bcasts.add())
                        lows.add()
                        nc.vector.tensor_tensor(scaled[h % 2][:], bcast_ps[h % 2][:, 0:T], flat(head_o, 4 * i + h),
                                                ALU.mult).then_inc(head_scaled, 1)
                        if h:
                            head_low((4 * i + h - 1, (h - 1) % 2))
                    gate_tile(c)
                head_low((4 * i + 3, 1))
            for c in range(2):
                split(2 * c + LEAD)
                split(2 * c + LEAD + 1)
                gate_tile(c)

            with loop(KT // 2, 2, [0, 1], {steps: 4}) as i:
                for c in range(2):
                    split(2 * c + LEAD)
                    split(2 * c + LEAD + 1)
                    v = finished(c)
                    j = 2 * i + c
                    nc.vector.tensor_tensor(blend[:], acc[c][:, 0:T], flat(gate_a, j), ALU.mult).then_inc(acc_read[c], 1)
                    dve.wait_ge(acc_read[c], v)
                    dve.wait_ge(vec_step, step(nc.vector.tensor_tensor(blend2[:], blend[:], flat(conv_part, j), ALU.add)))
                    dve.wait_ge(vec_step, step(nc.vector.tensor_copy(flat(mixed_h, j), blend2[:])))
                    nc.vector.tensor_tensor(flat(mixed_l, j), blend2[:], flat(mixed_h, j).bitcast(F32),
                                            ALU.subtract).then_inc(mixed_ready, 1)

            added = Tally(2)

            def add_square(slot):
                dve.wait_ge(squares_made, squares_in.add())
                nc.vector.tensor_tensor(square_sum[:], square_sum[:], square[slot][:], ALU.add).then_inc(squares_read, 1)
                dve.wait_ge(squares_read, added.add())

            dve.wait_ge(vec_step, step(nc.vector.memset(square_sum[:], 0.0)))
            with loop(KT // 2, 2, [0, 1], {squares_in: 2, added: 2}):
                for c in range(2):
                    split(2 * c + LEAD)
                    split(2 * c + LEAD + 1)
                    finished(c, wait=False)
                    add_square(c)

            def add_normed(dst, src, signal):
                view = "p (a t) -> p a t"
                for q in range(4):
                    dve.wait_ge(vec_step, step(nc.vector.tensor_tensor(
                        quarter(src, q).rearrange(view, a=QUARTER), quarter(src, q).rearrange(view, a=QUARTER),
                        over_quarter(rstd), ALU.mult)))
                    nc.vector.tensor_tensor(quarter(dst, q), quarter(x, q), quarter(src, q), ALU.add).then_inc(signal, 1)

            reciprocal_root()
            view = "p (a t) -> p a t"
            for q in range(5):
                if q < 4:
                    dve.wait_ge(vec_step, step(nc.vector.tensor_tensor(
                        quarter(mix_out, q).rearrange(view, a=QUARTER), quarter(mix_out, q).rearrange(view, a=QUARTER),
                        over_quarter(rstd), ALU.mult)))
                    nc.vector.tensor_tensor(quarter(x, q), quarter(x, q), quarter(mix_out, q), ALU.add
                                            ).then_inc(resid_made, 1)
                if q:
                    gained_low(q - 1)
            for q in range(4):
                add_quarter(q)
            fold_squares()

            used = Tally(1)

            def up_taps(j, c, dst):
                dve.wait_ge(tap_ready, taps.add())
                dve.wait_ge(vec_step, step(nc.vector.scalar_tensor_tensor(
                    dst[:, 1:T], up_raw[c][:, 0:T - 1], par[:, at(j + (P_UPCONV + 2 * FT + c * FT))], dst[:, 1:T],
                    ALU.mult, ALU.add)))
                return nc.vector.scalar_tensor_tensor(
                    dst[:, 2:T], up_raw[c][:, 0:T - 2], par[:, at(j + (P_UPCONV + c * FT))], dst[:, 2:T],
                    ALU.mult, ALU.add)

            def up_product():
                dve.wait_ge(silu_ready, silus.add())
                nc.vector.tensor_tensor(hidden[:], silu_a[:], up_b[:], ALU.mult).then_inc(hidden_read, 1)
                used.add()

            def up_parts(j):
                dve.wait_ge(hidden_read, used.value())
                dve.wait_ge(vec_step, step(nc.vector.tensor_copy(flat(hid_h, j), hidden[:])))
                nc.vector.tensor_tensor(flat(hid_l, j), hidden[:], flat(hid_h, j).bitcast(F32),
                                        ALU.subtract).then_inc(hidden_ready, 1)

            def up_pair(j, first):
                split(LEAD)
                if not first:
                    dve.wait_ge(vec_step, step(up_taps(j - 1, 1, up_b)))
                split(LEAD + 1)
                if first:
                    reciprocal_root()
                else:
                    up_product()
                scale_tokens(0, up_raw[0][:])
                split(LEAD + 2)
                up_taps(j, 0, up_a).then_inc(taps_made, 1)
                split(LEAD + 3)
                if not first:
                    up_parts(j - 1)
                scale_tokens(1, up_raw[1][:])

            up_pair(0, True)
            with loop(FT - 1, 2, [0, 1], {steps: 4, taps: 2, silus: 1, used: 1}) as j:
                up_pair(j + 1, False)

            def down_pair(first, last):
                for c in range(2):
                    for n in range(DOWN_SLABS):
                        m = c * DOWN_SLABS + n + LEAD
                        if not last or m < 2 * DOWN_SLABS:
                            split(m, DOWN_SIZES[m % DOWN_SLABS])
                        if first and c == 0 and n == 0:
                            dve.wait_ge(vec_step, step(up_taps(FT - 1, 1, up_b)))
                        if first and c == 0 and n == 1:
                            up_product()
                            up_parts(FT - 1)
                            dve.wait_ge(vec_step, step(nc.vector.memset(square_sum[:], 0.0)))
                    finished(c, DOWN_SLABS, wait=False)
                    add_square(c)
            down_pair(True, False)
            with repeat(dve, KT // 2 - 2, {slabs: 2 * DOWN_SLABS, cols: 2 * DOWN_SLABS, reads[0]: 1, reads[1]: 1,
                                           squares_in: 2, added: 2}):
                down_pair(False, False)
            down_pair(False, True)
            reciprocal_root()
            add_normed(down_out, down_out, out_made)

        @block.tensor
        def _(pe):
            slabs = Tally(RING)
            reads = [Tally() for _ in range(4)]
            merged, qruns, vreads, osq, diags = (Tally() for _ in range(5))
            scaled_heads = Tally(HEADS)

            def slab(n, out, rhs_h, rhs_l, k0, size, last_k, quarters=None):
                s = n % RING
                pe.wait_ge(low_ready, slabs.add())
                for b in range(size):
                    k = k0 + b
                    if quarters is not None and k % QUARTER == 0:
                        pe.wait_ge(gained_ready, quarters + k // QUARTER + 1)
                    nc.tensor.matmul(out, high[s][:, b, :], rhs_h[:, k, :], start=(k == 0), stop=False)
                    nc.tensor.matmul(out, high[s][:, b, :], rhs_l[:, k, :], start=False, stop=False)
                    done = nc.tensor.matmul(out, low[s][:, b, :], rhs_h[:, k, :], start=False, stop=(k == last_k))
                done.then_inc(slabs_used, 1)

            def col(n, slot, rhs, ready=None, extra=None, quarters=None):
                pe.wait_ge(acc_read[slot], reads[slot].add())
                for b in range(2):
                    if ready:
                        pe.wait_ge(ready[0], ready[1] + (b + 1) * SLAB)
                    slab(n + b, acc[slot][:, 0:T], rhs[0], rhs[1], b * SLAB, SLAB, KT - 1, quarters)
                    if extra:
                        extra(b)

            def loop(trips, n_cols, slots, more=None):
                per = {slabs: 2 * n_cols}
                for s in range(4):
                    per[reads[s]] = slots.count(s)
                per.update(more or {})
                return repeat(pe, trips, per)

            def channel_sum():
                nc.tensor.matmul(stat_ps[:, 0:T], ones[:], square_sum[:], start=True, stop=True).then_inc(sums_made, 1)

            pe.sem_inc(slabs_used, RING)
            pe.wait_ge(consts_made, 1)

            gained_hl, conv_hl, heads_hl = (gained_h, gained_l), (conv_h, conv_l), (heads_h, heads_l)
            mixed_hl, hid_hl = (mixed_h, mixed_l), (hid_h, hid_l)

            def mean_square(n):
                def extra(b):
                    if b == 0:
                        pe.wait_ge(square_sum_made, n)
                        channel_sum()
                return extra

            for c in range(6):
                col(2 * c, c % 3, gained_hl, None, mean_square(1) if c == 1 else None, 0 if c == 0 else None)
            with loop(KT // 2 - 1, 6, [0, 1, 2] * 2):
                for c in range(6):
                    col(2 * c, c % 3, gained_hl)
            with loop(KT, 2, [0, 1]):
                col(0, 0, gained_hl)
                col(2, 1, conv_hl, (conv_ready, 0))

            def score_level(s):
                if s == LEVELS:
                    done = nc.tensor.matmul(level_ps[:, 0:CHUNK], k_run[:, 0:CHUNK], q_run[:, CHUNK:T],
                                            start=True, stop=True)
                else:
                    h = 1 << s
                    keys = key if s == 0 else k_run
                    q = q_run[:].rearrange("p (c b u h) -> p c b u h", c=2, u=2, h=h)
                    for c in range(2):
                        done = nc.tensor.matmul(
                            level_ps[:, c * 64:c * 64 + 64].rearrange("p (b h) -> p b h", h=h),
                            keys[:, c * CHUNK:(c + 1) * CHUNK], q[:, c, :, 1, :], start=True, stop=True)
                done.then_inc(level_scored, 1)

            def head_extras(b, c, levels_on, out_on, head):
                s = 2 * c + b
                if s == 0 and out_on:
                    pe.wait_ge(level_merged, merged.add())
                    pe.wait_ge(v_ready, vreads.add())
                    nc.tensor.matmul(o_ps[:, 0:T], v_tok[:, 0, :], scores[:, 0:2, :].rearrange("p a t -> p (a t)"), start=True, stop=False)
                    nc.tensor.matmul(o_ps[:, CHUNK:T], v_tok[:, 1, :], scores[:, 2, :], start=False, stop=True
                                     ).then_inc(o_made, 1)
                if s == 0 and levels_on:
                    pe.wait_ge(q_run_ready, qruns.add())
                    for c2 in range(2):
                        t = slice(c2 * CHUNK, (c2 + 1) * CHUNK)
                        nc.tensor.matmul(level_ps[:, CHUNK + c2 * CHUNK:2 * CHUNK + c2 * CHUNK], key[:, t], query[:, t],
                                         start=True, stop=True)
                    score_level(0)
                if s == 1 and levels_on:
                    pe.wait_ge(acc_read[3], reads[3].value() + 1)
                    for c2 in range(2):
                        done = nc.tensor.transpose(v_ps[:, c2 * P:(c2 + 1) * P], v_chan[:, c2 * P:(c2 + 1) * P], ident[:])
                    done.then_inc(v_transposed, 1)
                if s > 0 and levels_on:
                    pe.wait_ge(level_merged, merged.add())
                    score_level(s)
                if s == 2 and out_on:
                    pe.wait_ge(o_squared, osq.add())
                    for half in range(2):
                        done = nc.tensor.matmul(stat_ps[:, at(head + half * HEADS)],
                                                o_square[:, half * P:(half + 1) * P], ones[:, 0:1],
                                                start=True, stop=True)
                    done.then_inc(head_summed, 1)

            def head(levels_on, out_on, i):
                for c in range(4):
                    col(2 * c, c, gained_hl, None, lambda b, c=c: head_extras(b, c, levels_on, out_on, i))

            head(False, False, None)
            head(True, False, None)
            with loop(HEADS - 2, 4, [0, 1, 2, 3], {merged: LEVELS + 1, qruns: 1, vreads: 1, osq: 1}) as i:
                head(True, True, i)
            head(True, True, HEADS - 2)
            for c in range(2):
                col(2 * c, c, gained_hl, None, lambda b, c=c: head_extras(b, c, False, True, HEADS - 1))
            with loop(4, 2, [0, 1], {diags: 4, scaled_heads: 4}):
                for c in range(2):
                    def spread(b, c=c):
                        h = 2 * c + b
                        pe.wait_ge(diag_ready, diags.add())
                        pe.wait_ge(head_scaled, scaled_heads.value() - 1)
                        scaled_heads.add()
                        nc.tensor.matmul(bcast_ps[h % 2][:, 0:T], ones[:], diag[h % 2][:].rearrange("p a b -> p (a b)"),
                                         start=True, stop=True).then_inc(head_bcast, 1)
                    col(2 * c, c, gained_hl, None, spread)
            for c in range(2):
                col(2 * c, c, gained_hl)
            with loop(KT // 2, 2, [0, 1]):
                for c in range(2):
                    col(2 * c, c, heads_hl, (heads_ready, 2))
            with loop(KT // 2, 2, [0, 1]):
                for c in range(2):
                    col(2 * c, c, mixed_hl, (mixed_ready, 0))
            pe.wait_ge(squares_read, 2 + KT)
            channel_sum()
            for c in range(2):
                col(2 * c, c, gained_hl, None, mean_square(2) if c == 1 else None, 4 if c == 0 else None)
            with loop(FT - 1, 2, [0, 1]):
                for c in range(2):
                    col(2 * c, c, gained_hl)
            with repeat(pe, KT // 2, {slabs: 2 * DOWN_SLABS, reads[0]: 1, reads[1]: 1}):
                for c in range(2):
                    pe.wait_ge(acc_read[c], reads[c].add())
                    for n in range(DOWN_SLABS):
                        if n in (0, DOWN_SLABS - 1):
                            pe.wait_ge(hidden_ready, SLAB * (DOWN_SLABS - 1) if n == 0 else FT)
                        slab(c * DOWN_SLABS + n, acc[c][:, 0:T], hid_hl[0], hid_hl[1], n * SLAB, DOWN_SIZES[n], FT - 1)
            pe.wait_ge(squares_read, 2 + 2 * KT)
            channel_sum()


def kernel(**inputs):
    import concourse.bacc as bacc
    from concourse.bass_utils import run_bass_kernel_spmd

    a = {k: np.asarray(v) for k, v in inputs.items()}

    def slabs(w):
        n = w.shape[1] // P
        return w.reshape(KT // SLAB, SLAB, P, n, P).transpose(3, 0, 2, 1, 4)

    names = ("q", "f", "i", "g", "cb", "cc", "ch", "ga", "gb")
    w_in = slabs(a["w_in"][0])
    w = {name: w_in[n * KT:(n + 1) * KT] for n, name in enumerate(names)}
    w["sc_out"], w["hg_out"], w["mix"] = (slabs(a[n][0]) for n in ("w_sc_out", "w_hg_out", "w_mix_out"))
    up = slabs(a["w_ffn_up"][0])
    w["up_a"], w["up_b"] = up[:FT], up[FT:]
    w_main = np.empty((COLS_MAIN, KT // SLAB, P, SLAB, P), np.float32)
    start = 0
    for group in (("cc", "ch", "cb"), ("gb", "sc_out"), ("f", "q", "g", "i"), ("ga",), ("hg_out",), ("mix",),
                  ("up_a", "up_b")):
        n = len(w[group[0]])
        for m, name in enumerate(group):
            w_main[start + m:start + n * len(group):len(group)] = w[name]
        start += n * len(group)
    w_main = w_main.reshape(SLABS_MAIN, P, SLAB, P)
    w_down = np.ascontiguousarray(a["w_ffn_down"][0].reshape(FT, P, KT, P).transpose(2, 1, 0, 3))

    def channels(v):
        return v.reshape(-1, P).T

    params = np.ascontiguousarray(np.concatenate([channels(v) for v in (
        a["norm_mix_pre"][0], a["norm_mix_post"][0], a["norm_ffn_pre"][0], a["norm_ffn_post"][0],
        a["hg_lower_bounds"][0], a["hg_out_norm"][0], a["sc_conv"][0], a["ffn_conv"][0], a["ffn_conv_bias"][0])], axis=1))

    def tiles(v):
        return np.ascontiguousarray(v.T.reshape(KT, P, T).transpose(1, 0, 2))

    ident = np.eye(P, dtype=np.float32)
    masks = np.zeros((P, LEVELS, CHUNK // 2), np.float32)
    for lv in range(LEVELS):
        h = 1 << lv
        for s in range(P):
            if s % (2 * h) < h:
                b = s // (2 * h)
                masks[s, lv, b * h:(b + 1) * h] = 1

    nc = bacc.Bacc("TRN2", target_bir_lowering=False, num_devices=1)
    arrays = {"xT": tiles(a["x"][0]), "params": params, "ident_c": ident, "masks_c": masks,
              "w_main": w_main, "w_down": w_down}
    aps = [nc.dram_tensor(n, list(v.shape), mybir.dt.from_np(v.dtype), kind="ExternalInput").ap() for n, v in arrays.items()]
    out = nc.dram_tensor("outT", [P, KT, T], F32, kind="ExternalOutput").ap()
    build(nc, *aps, out)
    r = run_bass_kernel_spmd(nc, [arrays], core_ids=[0])
    y = np.asarray(r.results[0]["outT"])
    return np.ascontiguousarray(y.transpose(2, 1, 0).reshape(1, T, D_MODEL))
```

```python
from contextlib import ExitStack, contextmanager

import numpy as np

import concourse.bass as bass
from concourse import mybir

P = 128
D_MODEL = 2048
T = 256
HEADS = 16
FFN = 5632
KT = D_MODEL // P
FT = FFN // P
CHUNK = 128
LEVELS = 7
QUARTER = KT // 4
QUARTERS = [(q * QUARTER, (q + 1) * QUARTER) for q in range(4)]
PARTS = [(0, QUARTER // 2), (QUARTER // 2, QUARTER)] + QUARTERS[1:]
PARTS_OUT = QUARTERS[:3] + [(3 * QUARTER, KT - 2), (KT - 2, KT)]
EPS = 1e-6
F_MIN = 1e-30

SLAB = 8
RING = 4
LEAD = 3
COLS_MAIN = 9 * KT + 3 * KT + 2 * FT
SLABS_MAIN = COLS_MAIN * KT // SLAB
DOWN_SIZES = [SLAB] * (FT // SLAB) + [FT % SLAB]
DOWN_SLABS = len(DOWN_SIZES)

P_MIX_PRE, P_MIX_POST, P_FFN_PRE, P_FFN_POST, P_LOWER = (KT * n for n in range(5))
P_HEAD_NORM = 5 * KT
P_CONV = P_HEAD_NORM + 1
P_UPCONV = P_CONV + 3 * KT
P_UPBIAS = P_UPCONV + 3 * 2 * FT
N_PARAMS = P_UPBIAS + 2 * FT

F32 = mybir.dt.float32
F32R = mybir.dt.float32r
U8 = mybir.dt.uint8
ACT = mybir.ActivationFunctionType
ALU = mybir.AluOpType


class Tally:

    def __init__(self, n=0):
        self.n, self.trip = n, 0

    def add(self, k=1):
        self.n += k
        return self.value()

    def value(self):
        return self.trip + self.n


@contextmanager
def repeat(eng, trips, per_trip):
    before = {t: t.n for t in per_trip}
    with eng.Fori(0, trips) as i:
        for t, k in per_trip.items():
            t.trip = i * k
        yield i
    for t, k in per_trip.items():
        assert t.n - before[t] == k, (t.n - before[t], k)
        t.trip = 0
        t.n += k * (trips - 1)


def at(i, c=1):
    return bass.ds(i, c)


def build(nc, xT, params, ident_d, masks_d, w_main, w_down, outT):
    ctx = ExitStack()
    with ctx:
        BASE = 16512
        KB = 1024

        def sb(name, shape, dt, off):
            return nc.alloc_sbuf_tensor_at(name, [P] + shape, dt, offset=BASE + off)

        tile_b = T * 4
        act_b = KT * tile_b
        gained_h = sb("gained_h", [KT, T], F32R, 0)
        gained_l = sb("gained_l", [KT, T], F32R, act_b)
        down_out = sb("down_out", [KT, T], F32, 0)
        squares = sb("squares", [4, QUARTER * T], F32, 48 * KB)
        gained = sb("gained", [KT, T], F32, 112 * KB)
        conv_h = sb("conv_h", [KT, T], F32R, 32 * KB)
        conv_l = sb("conv_l", [KT, T], F32R, 48 * KB)
        heads_h = sb("heads_h", [KT, T], F32R, 32 * KB)
        heads_l = sb("heads_l", [KT, T], F32R, 48 * KB)
        mix_out = sb("mix_out", [KT, T], F32, 32 * KB)
        head_o = sb("head_o", [HEADS, T], F32, 64 * KB)
        masks_f = sb("masks_f", [LEVELS, CHUNK // 2], F32, 64 * KB)
        head_g = sb("head_g", [HEADS, T], F32, 80 * KB)
        mixed_h = sb("mixed_h", [KT, T], F32R, 64 * KB)
        mixed_l = sb("mixed_l", [KT, T], F32R, 80 * KB)
        conv_part = sb("conv_part", [KT, T], F32, 96 * KB)
        gate_a = sb("gate_a", [KT, T], F32, 112 * KB)
        hid_h = sb("hid_h", [FT, T], F32R, 32 * KB)
        hid_l = sb("hid_l", [FT, T], F32R, 76 * KB)
        x = sb("x", [KT, T], F32, 128 * KB)
        raw = [sb(f"raw{s}", [SLAB, P], F32, (144 + 4 * s) * KB) for s in range(RING)]
        high = [sb(f"high{s}", [SLAB, P], F32R, (160 + 4 * s) * KB) for s in range(RING)]
        low = [sb(f"low{s}", [SLAB, P], F32R, (176 + 4 * s) * KB) for s in range(RING)]
        off = 192 * KB
        par = sb("par", [N_PARAMS], F32, off); off += -(-N_PARAMS * 4 // 32) * 32
        ident = sb("ident", [P], F32, off); off += P * 4
        ones = sb("ones", [P], F32, off); off += P * 4
        masks = sb("masks", [LEVELS, 2, CHUNK // 2], U8, off); off += LEVELS * CHUNK
        eps = sb("eps", [1], F32, off); off += 32
        lower = sb("lower", [KT], F32, off); off += KT * 4
        upper = sb("upper", [KT], F32, off); off += KT * 4
        neg_upper = sb("neg_upper", [KT], F32, off); off += KT * 4
        warm = sb("warm", [1], F32, off); off += 32
        head_r = sb("head_r", [2, HEADS], F32, off); off += 2 * HEADS * 4
        G = off
        slot = tile_b + 32
        assert BASE + G + 10 * slot <= 229344, BASE + G + 10 * slot

        def work(name, n, dt=F32, cols=T):
            return sb(name, [cols], dt, G + n * slot)

        ch_cc = work("ch_cc", 0, cols=T + 2)
        cc = work("cc", 1)
        conv_u = work("conv_u", 2)
        conv_y = work("conv_y", 3)
        gate_b = work("gate_b", 4)
        gate_in = [work("gate_in0", 7), work("gate_in1", 6)]
        rstd2 = work("rstd2", 5)
        square = [work("square0", 5), work("square1", 6)]
        square_sum = work("square_sum", 7)
        root = work("root", 8)
        rstd = work("rstd", 9)
        scaled = [work("scaled0", 3), work("scaled1", 4)]
        diag = [sb(f"diag{n}", [2, P], F32, G + n * slot) for n in range(2)]
        blend = work("blend", 2)
        blend2 = work("blend2", 3)
        up_raw = [work("up_raw0", 4), work("up_raw1", 5)]
        up_a = work("up_a", 0)
        up_b = work("up_b", 1)
        silu_a = work("silu_a", 2)
        hidden = work("hidden", 3)

        R = 32 * KB
        def rec(name, n, shape):
            return sb(name, shape, F32, R + n * KB)
        f_sig = rec("f_sig", 0, [T])
        f_gate = rec("f_gate", 1, [T])
        key = rec("key", 2, [T])
        q_sig = rec("q_sig", 3, [T])
        first_q = rec("first_q", 17, [2, CHUNK + CHUNK // 2])
        query = first_q[:, :, 0:CHUNK]
        q_run = rec("q_run", 5, [T])
        k_run = rec("k_run", 6, [T])
        v_chan = rec("v_chan", 7, [T])
        g_sig = rec("g_sig", 8, [T])
        totals = rec("totals", 9, [T])
        v_tok = rec("v_tok", 10, [2, P])
        o_square = rec("o_square", 11, [T])
        f_in = rec("f_in", 14, [T])
        q_in = rec("q_in", 15, [T])
        g_in = rec("g_in", 16, [T])
        scores = rec("scores", 12, [3, CHUNK])

        acc = [nc.alloc_psum_tensor(f"acc{n}", [P, 512], F32) for n in range(4)]
        level_ps = nc.alloc_psum_tensor("level_ps", [P, 512], F32)
        o_ps = nc.alloc_psum_tensor("o_ps", [P, 512], F32)
        v_ps = nc.alloc_psum_tensor("v_ps", [P, 512], F32)
        stat_ps = nc.alloc_psum_tensor("stat_ps", [P, 512], F32)
        bcast_ps = [level_ps, o_ps]

        def sem(name):
            return nc.alloc_semaphore(name)

        x_loaded = [sem(f"x_loaded{n}") for n in range(len(PARTS))]
        params_loaded = sem("params_loaded")
        consts_loaded = sem("consts_loaded")
        raw_loaded = [sem(f"raw_loaded{s}") for s in range(RING)]
        high_ready = sem("high_ready")
        low_ready = sem("low_ready")
        slabs_used = sem("slabs_used")
        acc_read = [sem(f"acc_read{n}") for n in range(4)]
        vec_step = sem("vec_step")
        bound_shifted = sem("bound_shifted")
        bound_exp = sem("bound_exp")
        consts_made = sem("consts_made")
        squares_made = sem("squares_made")
        squares_read = sem("squares_read")
        quarters_squared = sem("quarters_squared")
        gained_made = sem("gained_made")
        gained_high = sem("gained_high")
        gained_ready = sem("gained_ready")
        square_sum_made = sem("square_sum_made")
        sums_made = sem("sums_made")
        root_made = sem("root_made")
        rstd_made = sem("rstd_made")
        resid_made = sem("resid_made")
        conv_ready = sem("conv_ready")
        gate_ready = sem("gate_ready")
        key_ready = sem("key_ready")
        f_sig_ready = sem("f_sig_ready")
        q_sig_ready = sem("q_sig_ready")
        g_sig_ready = sem("g_sig_ready")
        k_run_ready = sem("k_run_ready")
        q_run_ready = sem("q_run_ready")
        level_scored = sem("level_scored")
        level_merged = sem("level_merged")
        v_transposed = sem("v_transposed")
        v_ready = sem("v_ready")
        o_made = sem("o_made")
        o_squared = sem("o_squared")
        head_summed = sem("head_summed")
        diag_ready = sem("diag_ready")
        head_bcast = sem("head_bcast")
        head_scaled = sem("head_scaled")
        heads_high = sem("heads_high")
        heads_ready = sem("heads_ready")
        mixed_ready = sem("mixed_ready")
        up_scaled = sem("up_scaled")
        taps_made = sem("taps_made")
        tap_ready = sem("tap_ready")
        silu_ready = sem("silu_ready")
        hidden_read = sem("hidden_read")
        hidden_ready = sem("hidden_ready")
        out_made = sem("out_made")
        stored = sem("stored")

        block = ctx.enter_context(nc.Block())

        @block.sync
        def _(sp):
            def first_slab(s):
                sp.dma_start(raw[s][:], w_main[s]).then_inc(raw_loaded[s], 16)

            sp.dma_start(par[:], params).then_inc(params_loaded, 16)
            for n, (a, b) in enumerate(PARTS):
                sp.dma_start(x[:, a:b, :], xT[:, a:b, :]).then_inc(x_loaded[n], 16)
                if n < RING:
                    first_slab(n)
            sp.dma_start(ident[:], ident_d).then_inc(consts_loaded, 16)
            sp.dma_start(masks_f[:], masks_d).then_inc(consts_loaded, 16)
            freed = Tally(RING)
            with repeat(sp, SLABS_MAIN // RING - 1, {freed: RING}) as i:
                for s in range(RING):
                    sp.wait_ge(low_ready, freed.add())
                    sp.dma_start(raw[s][:], w_main[at((i + 1) * RING + s), :, :, :].rearrange("o p k c -> p (o k) c")
                                 ).then_inc(raw_loaded[s], 16)
            with repeat(sp, KT // 2, {freed: 2 * DOWN_SLABS}) as i:
                for m in range(2 * DOWN_SLABS):
                    n = m % DOWN_SLABS
                    sp.wait_ge(low_ready, freed.add())
                    sp.dma_start(raw[m % RING][:, 0:DOWN_SIZES[n], :],
                                 w_down[at(2 * i + m // DOWN_SLABS), :, n * SLAB:n * SLAB + DOWN_SIZES[n], :]
                                 .rearrange("o p k c -> p (o k) c")).then_inc(raw_loaded[m % RING], 16)
            for n, (a, b) in enumerate(PARTS_OUT):
                sp.wait_ge(out_made, n + 1)
                sp.dma_start(outT[:, a:b, :], down_out[:, a:b, :]).then_inc(stored, 16)
            sp.wait_ge(stored, 16 * len(PARTS_OUT))

        @block.scalar
        def _(act):
            slabs = Tally()
            loads = [Tally() for _ in range(RING)]
            cols = Tally(RING)
            reads = [Tally(1) for _ in range(4)]
            squares_out = Tally(2)
            keys, sums, levels, outs, vts, gained_q, resid = (Tally() for _ in range(7))

            def split(n, size=SLAB):
                s = n % RING
                act.wait_ge(raw_loaded[s], loads[s].add(16))
                act.wait_ge(slabs_used, slabs.add())
                nc.scalar.activation(high[s][:, 0:size, :], raw[s][:, 0:size, :], ACT.Copy).then_inc(high_ready, 1)

            def finished(slot, n=2, wait=True):
                v = cols.add(n)
                if wait:
                    act.wait_ge(slabs_used, v)
                reads[slot].add()

            def scaled_in(slot):
                cols.add(2)
                act.wait_ge(acc_read[slot], reads[slot].add())

            def part(t, a, b):
                return t[:, a:b, :].rearrange("p a t -> p (a t)")

            def times_gain(a, b, gain):
                for k in range(a, b):
                    done = nc.scalar.activation(gained[:, k, :], x[:, k, :], ACT.Copy,
                                                scale=par[:, gain + k:gain + k + 1])
                done.then_inc(gained_made, 1)

            def gained_parts(a, b):
                act.wait_ge(gained_made, gained_q.add())
                nc.scalar.activation(part(gained_h, a, b), part(gained, a, b), ACT.Copy).then_inc(gained_high, 1)

            def quarter_squares(q):
                nc.scalar.activation(squares[:, q, :], part(x, q * QUARTER, (q + 1) * QUARTER), ACT.Square).then_inc(quarters_squared, 1)

            def loop(trips, n_cols, slots, more=None):
                n = 2 * n_cols
                per = {slabs: n, cols: n}
                for s in range(RING):
                    per[loads[s]] = 16 * n // RING
                for s in range(4):
                    per[reads[s]] = slots.count(s)
                per.update(more or {})
                return repeat(act, trips, per)

            def root_of(ps, out, scale):
                act.wait_ge(sums_made, sums.add())
                nc.scalar.activation(out, ps, ACT.Sqrt, bias=eps[:], scale=scale).then_inc(root_made, 1)

            act.wait_ge(consts_made, 2)
            nc.scalar.activation(warm[:], eps[:], ACT.Sqrt)
            gained_parts(*PARTS[0])
            split(0)
            split(1)
            gained_parts(*PARTS[1])
            quarter_squares(0)
            gained_parts(*PARTS[2])
            split(2)
            gained_parts(*PARTS[3])
            split(3)
            quarter_squares(1)
            act.wait_ge(x_loaded[4], 16)
            act.wait_ge(params_loaded, 16)
            times_gain(*PARTS[4], P_MIX_PRE)
            gained_parts(*PARTS[4])
            quarter_squares(2)
            quarter_squares(3)

            def conv_pair(first):
                for c in range(6):
                    if not (first and c == 0):
                        split(2 * c + LEAD)
                    if first and c == 2:
                        root_of(stat_ps[:, 0:T], root[:], 1.0 / D_MODEL)
                    split(2 * c + LEAD + 1)
                    finished(c % 3, 2 if not first or c > 1 else 3 if c == 0 else 1, wait=c % 3 == 0)
                    if c % 3 == 0:
                        act.wait_ge(acc_read[1], reads[1].value())
                        nc.scalar.activation(cc[:], acc[0][:, 0:T], ACT.Copy).then_inc(acc_read[0], 1)
                if first:
                    act.wait_ge(bound_shifted, 1)
                    nc.scalar.activation(neg_upper[:], lower[:], ACT.Exp).then_inc(bound_exp, 1)

            conv_pair(True)
            with loop(KT // 2 - 1, 6, [0, 1, 2] * 2):
                conv_pair(False)

            nc.scalar.activation(warm[:], eps[:], ACT.Sigmoid)
            with loop(KT, 2, [0, 1]) as j:
                split(LEAD)
                split(LEAD + 1)
                scaled_in(0)
                nc.scalar.activation(gate_b[:], gate_in[0][:], ACT.Sigmoid).then_inc(gate_ready, 1)
                split(LEAD + 2)
                split(LEAD + 3)
                finished(1, wait=False)

            def head_extra_a(out_on):
                if out_on:
                    act.wait_ge(o_made, outs.add())
                    nc.scalar.activation(o_square[:], o_ps[:, 0:T], ACT.Square).then_inc(o_squared, 1)

            def head_extra_b(levels_on):
                if levels_on:
                    act.wait_ge(v_transposed, vts.add())
                    nc.scalar.activation(v_tok[:], v_ps[:, 0:T].rearrange("p (a b) -> p a b", a=2),
                                         ACT.Copy).then_inc(v_ready, 1)

            def head(levels_on, out_on):
                split(LEAD)
                head_extra_a(out_on)
                split(LEAD + 1)
                head_extra_b(levels_on)
                scaled_in(0)
                nc.scalar.activation(f_sig[:], f_in[:], ACT.Sigmoid).then_inc(f_sig_ready, 1)
                split(LEAD + 2)
                split(LEAD + 3)
                scaled_in(1)
                nc.scalar.activation(q_sig[:], q_in[:], ACT.Sigmoid).then_inc(q_sig_ready, 1)
                split(LEAD + 4)
                split(LEAD + 5)
                scaled_in(2)
                nc.scalar.activation(g_sig[:], g_in[:], ACT.Sigmoid).then_inc(g_sig_ready, 1)
                split(LEAD + 6)
                split(LEAD + 7)
                finished(3, wait=False)
                act.wait_ge(key_ready, keys.add())
                if levels_on:
                    act.wait_ge(level_scored, levels.add(LEVELS + 1))
                nc.scalar.activation(k_run[:], key[:], ACT.Copy).then_inc(k_run_ready, 1)

            head(False, False)
            head(True, False)
            with loop(HEADS - 2, 4, [0, 1, 2, 3], {keys: 1, levels: LEVELS + 1, outs: 1, vts: 1}):
                head(True, True)

            def gate_tile(slot, j):
                scaled_in(slot)
                nc.scalar.activation(gate_a[:, at(j), :].rearrange("p a t -> p (a t)"), gate_in[slot % 2][:],
                                     ACT.Sigmoid).then_inc(gate_ready, 1)

            for c in range(4):
                split(2 * c + LEAD)
                if c == 0:
                    head_extra_a(True)
                split(2 * c + LEAD + 1)
                if c == 0:
                    head_extra_b(True)
                gate_tile(c, c)
            split(LEAD)
            head_extra_a(True)
            split(LEAD + 1)
            gate_tile(0, 4)
            split(LEAD + 2)
            split(LEAD + 3)
            gate_tile(1, 5)
            split(LEAD)
            act.wait_ge(head_summed, HEADS)
            nc.scalar.activation(head_r[:], stat_ps[:, 0:2 * HEADS].rearrange("p (a b) -> p a b", a=2),
                                 ACT.Sqrt, bias=eps[:], scale=1.0 / P).then_inc(root_made, 1)
            split(LEAD + 1)
            gate_tile(0, 6)
            split(LEAD + 2)
            split(LEAD + 3)
            gate_tile(1, 7)
            scaleds = Tally(HEADS)

            def spread_roots(i, h):
                for half in range(2):
                    done = nc.scalar.activation(diag[h % 2][:, half, :], ident[:], ACT.Copy,
                                                scale=head_r[:, half, at(4 * i + h)])
                done.then_inc(diag_ready, 1)

            def head_high(i, h):
                act.wait_ge(head_scaled, scaleds.add())
                nc.scalar.activation(heads_h[:, at(4 * i + h), :].rearrange("p a t -> p (a t)"),
                                     scaled[h % 2][:], ACT.Copy).then_inc(heads_high, 1)

            def norm_four(i, last):
                for c in range(2):
                    for b in range(2):
                        h = 2 * c + b
                        split(h + LEAD)
                        if h:
                            head_high(i, h - 1)
                        if not (last and h == 3):
                            spread_roots(i, h + 1)
                    gate_tile(c, 2 * i + 8 + c)
                head_high(i, 3)

            act.wait_ge(rstd_made, 2)
            spread_roots(0, 0)
            with loop(3, 2, [0, 1], {scaleds: 4}) as i:
                norm_four(i, False)
            norm_four(3, True)

            with loop(KT // 2, 2, [0, 1]):
                for c in range(2):
                    split(2 * c + LEAD)
                    split(2 * c + LEAD + 1)
                    finished(c, wait=False)

            def out_tile(dst, slot, j, gain):
                act.wait_ge(squares_read, squares_out.value() - 1)
                squares_out.add()
                nc.scalar.activation(square[slot][:], acc[slot][:, 0:T], ACT.Square).then_inc(squares_made, 1)
                nc.scalar.activation(dst[:, at(j), :].rearrange("p a t -> p (a t)"), acc[slot][:, 0:T], ACT.Copy,
                                     scale=par[:, at(j + gain)]).then_inc(acc_read[slot], 1)

            nc.scalar.activation(warm[:], eps[:], ACT.Sqrt)
            with loop(KT // 2, 2, [0, 1], {squares_out: 2}) as i:
                for c in range(2):
                    split(2 * c + LEAD)
                    split(2 * c + LEAD + 1)
                    finished(c)
                    out_tile(mix_out, c, 2 * i + c, P_MIX_POST)
            split(LEAD)
            root_of(stat_ps[:, 0:T], root[:], 1.0 / D_MODEL)
            for a, b in PARTS:
                act.wait_ge(resid_made, resid.add())
                times_gain(a, b, P_FFN_PRE)
                gained_parts(a, b)
            for q in range(4):
                if q % 2 == 0:
                    split(LEAD + 1 + q // 2)
                quarter_squares(q)

            used = Tally(1)
            a_taps = Tally()

            def tap(j, c, dst, slot=None):
                scaled_in(c if slot is None else slot)
                if c == 0:
                    act.wait_ge(hidden_read, used.add() - 1)
                first_tap(j, c, dst)

            def first_tap(j, c, dst):
                nc.scalar.activation(dst[:], up_raw[c][:], ACT.Identity, bias=par[:, at(j + (P_UPBIAS + c * FT))],
                                     scale=par[:, at(j + (P_UPCONV + 4 * FT + c * FT))]).then_inc(tap_ready, 1)

            def up_silu():
                act.wait_ge(taps_made, a_taps.add())
                nc.scalar.activation(silu_a[:], up_a[:], ACT.Silu).then_inc(silu_ready, 1)

            def up_pair(j, slot=None):
                split(LEAD)
                tap(j - 1, 1, up_b, slot)
                split(LEAD + 1)
                split(LEAD + 2)
                tap(j, 0, up_a)
                split(LEAD + 3)
                up_silu()

            for c in range(2):
                finished(c, 3 - 2 * c)
                nc.scalar.activation(up_raw[c][:], acc[c][:, 0:T], ACT.Copy).then_inc(acc_read[c], 1)
            split(LEAD + 3)
            for n in range(3):
                split(LEAD + n)
            root_of(stat_ps[:, 0:T], root[:], 1.0 / D_MODEL)
            used.add()
            act.wait_ge(up_scaled, 1)
            first_tap(0, 0, up_a)
            act.wait_ge(up_scaled, 2)
            first_tap(0, 1, up_b)
            up_silu()
            split(LEAD + 3)
            tap(1, 0, up_a, 2)
            up_silu()
            up_pair(2, 3)
            with loop(FT - 3, 2, [0, 1], {used: 1, a_taps: 1}) as j:
                up_pair(j + 3)

            per = {slabs: 2 * DOWN_SLABS, cols: 2 * DOWN_SLABS, reads[0]: 1, reads[1]: 1, squares_out: 2}
            for s in range(RING):
                per[loads[s]] = 16 * 2 * DOWN_SLABS // RING

            def down_pair(i, first, last):
                for c in range(2):
                    for n in range(DOWN_SLABS):
                        m = c * DOWN_SLABS + n + LEAD
                        if not last or m < 2 * DOWN_SLABS:
                            split(m, DOWN_SIZES[m % DOWN_SLABS])
                        if first and c == 0 and n == 0:
                            tap(FT - 1, 1, up_b)
                            nc.scalar.activation(warm[:], eps[:], ACT.Sqrt)
                    finished(c, DOWN_SLABS)
                    out_tile(down_out, c, 2 * i + c, P_FFN_POST)
            down_pair(0, True, False)
            with repeat(act, KT // 2 - 2, per) as i:
                down_pair(i + 1, False, False)
            down_pair(KT // 2 - 1, False, True)
            root_of(stat_ps[:, 0:T], root[:], 1.0 / D_MODEL)

        @block.vector
        def _(dve):
            slabs = Tally()
            cols = Tally(RING)
            reads = [Tally(1) for _ in range(4)]
            steps = Tally()
            (squares_in, roots, fs, qs, gs, krs, scored, outs, bcasts, highs, taps, silus, gates, gained_q, quarter_sq,
             rstds) = (Tally() for _ in range(16))
            gate_outs = Tally(-1)

            def step(ins):
                ins.then_inc(vec_step, 1)
                return steps.add()

            def split(n, size=SLAB):
                s = n % RING
                dve.wait_ge(high_ready, slabs.add())
                nc.vector.tensor_tensor(low[s][:, 0:size, :], raw[s][:, 0:size, :], high[s][:, 0:size, :].bitcast(F32),
                                        ALU.subtract).then_inc(low_ready, 1)

            def finished(slot, n=2, wait=True):
                v = cols.add(n)
                if wait:
                    dve.wait_ge(slabs_used, v)
                return reads[slot].add()

            def loop(trips, n_cols, slots, more=None):
                per = {slabs: 2 * n_cols, cols: 2 * n_cols}
                for s in range(4):
                    per[reads[s]] = slots.count(s)
                per.update(more or {})
                return repeat(dve, trips, per)

            def flat(t, i):
                return t[:, at(i), :].rearrange("p a t -> p (a t)")

            def part(t, a, b):
                return t[:, a:b, :].rearrange("p a t -> p (a t)")

            def over_tiles(t, n):
                return t[:].rearrange("p (o t) -> p o t", o=1).broadcast_to([P, n, T])

            def reciprocal_root():
                dve.wait_ge(root_made, roots.add())
                nc.vector.reciprocal(rstd[:], root[:]).then_inc(rstd_made, 1)
                dve.wait_ge(rstd_made, rstds.add())

            def times_gain(n):
                dve.wait_ge(x_loaded[n], 16)
                for k in range(*PARTS[n]):
                    done = nc.vector.tensor_scalar(gained[:, k, :], x[:, k, :], par[:, P_MIX_PRE + k:P_MIX_PRE + k + 1],
                                                   None, ALU.mult)
                done.then_inc(gained_made, 1)

            def gained_low(a, b):
                dve.wait_ge(gained_high, gained_q.add())
                nc.vector.tensor_tensor(part(gained_l, a, b), part(gained, a, b), part(gained_h, a, b).bitcast(F32),
                                        ALU.subtract).then_inc(gained_ready, 1)

            def add_quarter(q):
                dve.wait_ge(quarters_squared, quarter_sq.add())
                if q:
                    dve.wait_ge(vec_step, step(nc.vector.tensor_tensor(squares[:, 0, :], squares[:, 0, :], squares[:, q, :],
                                                                       ALU.add)))

            def fold_squares():
                half = QUARTER * T // 2
                dve.wait_ge(vec_step, step(nc.vector.tensor_tensor(squares[:, 0, 0:half], squares[:, 0, 0:half],
                                                                   squares[:, 0, half:2 * half], ALU.add)))
                nc.vector.tensor_tensor(square_sum[:], squares[:, 0, 0:T], squares[:, 0, T:2 * T], ALU.add
                                        ).then_inc(square_sum_made, 1)

            def scale_tokens(slot, dst):
                finished(slot)
                nc.vector.tensor_tensor(dst, acc[slot][:, 0:T], rstd[:], ALU.mult).then_inc(acc_read[slot], 1)

            dve.sem_inc(low_ready, RING)
            for s in range(4):
                dve.sem_inc(acc_read[s], 1)
            dve.sem_inc(squares_read, 2)
            dve.sem_inc(hidden_read, 1)
            nc.vector.memset(ones[:], 1.0).then_inc(consts_made, 1)
            nc.vector.memset(eps[:], EPS).then_inc(consts_made, 1)
            step(nc.vector.memset(ch_cc[:, 0:2], 0.0))
            dve.wait_ge(params_loaded, 16)
            times_gain(0)
            gained_low(*PARTS[0])
            split(0)
            times_gain(1)
            split(1)
            gained_low(*PARTS[1])
            times_gain(2)
            times_gain(3)
            gained_low(*PARTS[2])
            split(2)
            gained_low(*PARTS[3])
            split(3)
            gained_low(*PARTS[4])
            add_quarter(0)
            add_quarter(1)
            split(LEAD + 1)
            add_quarter(2)
            split(LEAD + 2)
            add_quarter(3)
            fold_squares()
            lb = par[:, P_LOWER:P_LOWER + KT]
            nc.vector.tensor_tensor(lower[:], lb, lb, ALU.subtract).then_inc(bound_shifted, 1)

            def lower_bounds():
                dve.wait_ge(bound_exp, 1)
                dve.wait_ge(vec_step, step(nc.vector.reciprocal(upper[:], neg_upper[:])))
                dve.wait_ge(vec_step, step(nc.vector.tensor_tensor(neg_upper[:], neg_upper[:], upper[:], ALU.mult)))
                dve.wait_ge(vec_step, step(nc.vector.tensor_tensor(lower[:], neg_upper[:], neg_upper[:], ALU.subtract)))
                step(nc.vector.tensor_scalar(upper[:], lower[:], -1.0, 1.0, ALU.mult, ALU.add))
                dve.wait_ge(vec_step, step(nc.vector.tensor_scalar(neg_upper[:], lower[:], -1.0, None, ALU.add)))

            def conv_pair(i, first):
                for h in range(2):
                    j = 2 * i + h
                    base = 6 * h
                    early = first and h == 0
                    if not early:
                        if not first:
                            split(base + LEAD)
                        split(base + LEAD + 1)
                    cc_read = finished(0, 3 if early else 2, wait=False)
                    if not early:
                        split(base + LEAD + 2)
                        split(base + LEAD + 3)
                    else:
                        for n in range(3, 6):
                            split(LEAD + n)
                        reciprocal_root()
                        dve.wait_ge(vec_step, step(nc.vector.tensor_tensor(rstd2[:], rstd[:], rstd[:], ALU.mult)))
                    v = finished(1, 1 if early else 2)
                    dve.wait_ge(acc_read[0], cc_read)
                    nc.vector.tensor_tensor(ch_cc[:, 2:T + 2], acc[1][:, 0:T], cc[:], ALU.mult).then_inc(acc_read[1], 1)
                    if early:
                        split(LEAD + 6)
                    dve.wait_ge(acc_read[1], v)
                    dve.wait_ge(vec_step, step(nc.vector.tensor_tensor(ch_cc[:, 2:T + 2], ch_cc[:, 2:T + 2], rstd2[:],
                                                                       ALU.mult)))
                    tap = [par[:, at(j + (P_CONV + n * KT))] for n in range(3)]
                    dve.wait_ge(vec_step, step(nc.vector.tensor_scalar(conv_u[:], ch_cc[:, 2:T + 2], tap[2], None, ALU.mult)))
                    dve.wait_ge(vec_step, step(nc.vector.scalar_tensor_tensor(conv_u[:], ch_cc[:, 1:T + 1], tap[1],
                                                                              conv_u[:], ALU.mult, ALU.add)))
                    dve.wait_ge(vec_step, step(nc.vector.scalar_tensor_tensor(conv_u[:], ch_cc[:, 0:T], tap[0],
                                                                              conv_u[:], ALU.mult, ALU.add)))
                    step(nc.vector.tensor_tensor(conv_u[:], conv_u[:], rstd[:], ALU.mult))
                    if not early:
                        split(base + LEAD + 4)
                        split(base + LEAD + 5)
                    v = finished(2)
                    dve.wait_ge(vec_step, steps.value())
                    nc.vector.tensor_tensor(conv_y[:], acc[2][:, 0:T], conv_u[:], ALU.mult).then_inc(acc_read[2], 1)
                    dve.wait_ge(acc_read[2], v)
                    dve.wait_ge(vec_step, step(nc.vector.tensor_copy(flat(conv_h, j), conv_y[:])))
                    nc.vector.tensor_tensor(flat(conv_l, j), conv_y[:], flat(conv_h, j).bitcast(F32),
                                            ALU.subtract).then_inc(conv_ready, 1)

            conv_pair(0, True)
            lower_bounds()
            dve.wait_ge(consts_loaded, 32)
            for c in range(2):
                dve.wait_ge(vec_step, step(nc.vector.tensor_copy(masks[:, :, c, :], masks_f[:])))
            with loop(KT // 2 - 1, 6, [0, 1, 2] * 2, {steps: 12}) as i:
                conv_pair(i + 1, False)

            with loop(KT, 2, [0, 1], {gates: 1}) as j:
                split(LEAD)
                split(LEAD + 1)
                scale_tokens(0, gate_in[0][:])
                split(LEAD + 2)
                split(LEAD + 3)
                finished(1)
                dve.wait_ge(gate_ready, gates.add())
                nc.vector.tensor_tensor(flat(conv_part, j), acc[1][:, 0:T], gate_b[:], ALU.mult).then_inc(acc_read[1], 1)

            def total(level):
                if level == 0:
                    return f_gate[:]
                start = T - 2 * (T >> level)
                return totals[:, start:start + (T >> level)]

            def chunks(t):
                return t[:].rearrange("p (c t) -> p c t", c=2)

            def halves(t, h):
                return t[:].rearrange("p (b u h) -> p b u h", u=2, h=h)

            def merge(s):
                dve.wait_ge(level_scored, scored.add())
                if s == LEVELS:
                    nc.vector.tensor_copy(scores[:, 1, :], level_ps[:, 0:CHUNK]).then_inc(level_merged, 1)
                    return
                h = 1 << s
                products = level_ps[:, 0:CHUNK].rearrange("p (c t) -> p c t", c=2)
                if s == 0:
                    first = level_ps[:, CHUNK:4 * CHUNK].rearrange("p (c t) -> p c t", c=2)
                    products = first[:, :, CHUNK:]
                    dve.wait_ge(k_run_ready, krs.add())
                    v = step(nc.vector.tensor_tensor(
                        scores[:, 0:3:2, :], first[:, :, 0:CHUNK],
                        ident[:].rearrange("p (o t) -> p o t", o=1).broadcast_to([P, 2, CHUNK]), ALU.mult))
                tot = total(s).rearrange("p (b u o) -> p b u o", u=2, o=1)
                nb = T // (2 * h)
                nc.vector.tensor_tensor(halves(q_run, h)[:, :, 1, :], halves(q_run, h)[:, :, 1, :],
                                        tot[:, :, 0, :].broadcast_to([P, nb, h]), ALU.mult)
                nc.vector.tensor_tensor(halves(k_run, h)[:, :, 0, :], halves(k_run, h)[:, :, 0, :],
                                        tot[:, :, 1, :].broadcast_to([P, nb, h]), ALU.mult)
                if s == 0:
                    dve.wait_ge(vec_step, v)
                if s < LEVELS - 1:
                    t2 = total(s).rearrange("p (b u) -> p b u", u=2)
                    nc.vector.tensor_tensor(total(s + 1), t2[:, :, 0], t2[:, :, 1], ALU.mult)
                nc.vector.copy_predicated(
                    scores[:, 0:3:2, :].rearrange("p c (b u h) -> p c b u h", u=2, h=h)[:, :, :, 1, :],
                    masks[:, s, :, :].rearrange("p c (b h) -> p c b h", h=h),
                    products.rearrange("p c (b h) -> p c b h", h=h)).then_inc(level_merged, 1)

            def head_output(i):
                dve.wait_ge(o_squared, outs.add())
                nc.vector.tensor_tensor(flat(head_o, i), o_ps[:, 0:T], flat(head_g, i), ALU.mult).then_inc(head_scaled, 1)

            def head(i, levels_on, out_on):
                split(LEAD)
                if out_on:
                    head_output(i - 2)
                if levels_on:
                    merge(0)
                split(LEAD + 1)
                if levels_on:
                    merge(1)
                scale_tokens(0, f_in[:])
                split(LEAD + 2)
                if levels_on:
                    merge(2)
                dve.wait_ge(f_sig_ready, fs.add())
                dve.wait_ge(vec_step, step(nc.vector.tensor_scalar(f_gate[:], f_sig[:], upper[:, at(i)], lower[:, at(i)],
                                                                   ALU.mult, ALU.add)))
                step(nc.vector.tensor_scalar(f_gate[:], f_gate[:], F_MIN, None, ALU.max))
                nc.vector.tensor_scalar(key[:], f_sig[:], -1.0, neg_upper[:, at(i)], ALU.add, ALU.mult).then_inc(key_ready, 1)
                split(LEAD + 3)
                if levels_on:
                    merge(3)
                scale_tokens(1, q_in[:])
                split(LEAD + 4)
                if levels_on:
                    merge(4)
                dve.wait_ge(q_sig_ready, qs.add())
                step(nc.vector.tensor_tensor(query, chunks(q_in), chunks(q_sig), ALU.mult))
                split(LEAD + 5)
                if levels_on:
                    merge(5)
                scale_tokens(2, g_in[:])
                split(LEAD + 6)
                if levels_on:
                    merge(6)
                dve.wait_ge(g_sig_ready, gs.add())
                step(nc.vector.scalar_tensor_tensor(flat(head_g, i), g_in[:], par[:, P_HEAD_NORM:P_HEAD_NORM + 1],
                                                    g_sig[:], ALU.mult, ALU.mult))
                split(LEAD + 7)
                if levels_on:
                    merge(7)
                scale_tokens(3, v_chan[:])
                dve.wait_ge(vec_step, steps.value())
                nc.vector.tensor_tensor(chunks(q_run), query, chunks(f_gate), ALU.mult)
                nc.vector.tensor_tensor(first_q[:, :, CHUNK:], query[:, :, 1::2], chunks(f_gate)[:, :, 1::2], ALU.mult
                                        ).then_inc(q_run_ready, 1)

            head(0, False, False)
            head(1, True, False)
            with loop(HEADS - 2, 4, [0, 1, 2, 3],
                      {steps: 5, scored: LEVELS + 1, krs: 1, fs: 1, qs: 1, gs: 1, outs: 1}) as i:
                head(i + 2, True, True)

            def gate_tile(slot):
                dve.wait_ge(gate_ready, gate_outs.add())
                scale_tokens(slot, gate_in[slot % 2][:])

            gate_outs.add(KT - 1)
            for c in range(4):
                split(2 * c + LEAD)
                if c == 0:
                    head_output(HEADS - 2)
                merge(2 * c)
                split(2 * c + LEAD + 1)
                merge(2 * c + 1)
                gate_tile(c)
            split(LEAD)
            head_output(HEADS - 1)
            split(LEAD + 1)
            gate_tile(0)
            split(LEAD + 2)
            split(LEAD + 3)
            gate_tile(1)
            split(LEAD)
            split(LEAD + 1)
            dve.wait_ge(root_made, roots.add())
            nc.vector.reciprocal(head_r[:], head_r[:]).then_inc(rstd_made, 1)
            rstds.add()
            gate_tile(0)
            split(LEAD + 2)
            split(LEAD + 3)
            gate_tile(1)
            def head_low(i, h):
                dve.wait_ge(heads_high, highs.add())
                nc.vector.tensor_tensor(flat(heads_l, 4 * i + h), scaled[h % 2][:], flat(heads_h, 4 * i + h).bitcast(F32),
                                        ALU.subtract).then_inc(heads_ready, 1)

            lows = Tally(1)
            dve.sem_inc(heads_ready, 2)
            with loop(4, 2, [0, 1], {bcasts: 4, highs: 4, gate_outs: 2, lows: 4}) as i:
                for c in range(2):
                    for b in range(2):
                        h = 2 * c + b
                        split(2 * c + b + LEAD)
                        dve.wait_ge(heads_ready, lows.value())
                        dve.wait_ge(head_bcast, bcasts.add())
                        lows.add()
                        nc.vector.tensor_tensor(scaled[h % 2][:], bcast_ps[h % 2][:, 0:T], flat(head_o, 4 * i + h),
                                                ALU.mult).then_inc(head_scaled, 1)
                        if h:
                            head_low(i, h - 1)
                    gate_tile(c)
                head_low(i, 3)

            with loop(KT // 2, 2, [0, 1], {steps: 4}) as i:
                for c in range(2):
                    split(2 * c + LEAD)
                    split(2 * c + LEAD + 1)
                    v = finished(c)
                    j = 2 * i + c
                    nc.vector.tensor_tensor(blend[:], acc[c][:, 0:T], flat(gate_a, j), ALU.mult).then_inc(acc_read[c], 1)
                    dve.wait_ge(acc_read[c], v)
                    dve.wait_ge(vec_step, step(nc.vector.tensor_tensor(blend2[:], blend[:], flat(conv_part, j), ALU.add)))
                    dve.wait_ge(vec_step, step(nc.vector.tensor_copy(flat(mixed_h, j), blend2[:])))
                    nc.vector.tensor_tensor(flat(mixed_l, j), blend2[:], flat(mixed_h, j).bitcast(F32),
                                            ALU.subtract).then_inc(mixed_ready, 1)

            added = Tally(2)

            def add_square(slot):
                dve.wait_ge(squares_made, squares_in.add())
                nc.vector.tensor_tensor(square_sum[:], square_sum[:], square[slot][:], ALU.add).then_inc(squares_read, 1)
                dve.wait_ge(squares_read, added.add())

            dve.wait_ge(vec_step, step(nc.vector.memset(square_sum[:], 0.0)))
            with loop(KT // 2, 2, [0, 1], {squares_in: 2, added: 2}):
                for c in range(2):
                    split(2 * c + LEAD)
                    split(2 * c + LEAD + 1)
                    finished(c, wait=False)
                    add_square(c)

            def add_normed(dst, src, a, b, signal):
                dve.wait_ge(vec_step, step(nc.vector.tensor_tensor(src[:, a:b, :], src[:, a:b, :], over_tiles(rstd, b - a),
                                                                   ALU.mult)))
                nc.vector.tensor_tensor(part(dst, a, b), part(x, a, b), part(src, a, b), ALU.add).then_inc(signal, 1)

            split(LEAD)
            reciprocal_root()
            for n, (a, b) in enumerate(PARTS):
                add_normed(x, mix_out, a, b, resid_made)
                if n:
                    gained_low(*PARTS[n - 1])
            gained_low(*PARTS[-1])
            for q in range(4):
                if q % 2 == 0:
                    split(LEAD + 1 + q // 2)
                add_quarter(q)
            fold_squares()

            used = Tally(1)

            def up_taps(j, c, dst):
                dve.wait_ge(tap_ready, taps.add())
                dve.wait_ge(vec_step, step(nc.vector.scalar_tensor_tensor(
                    dst[:, 1:T], up_raw[c][:, 0:T - 1], par[:, at(j + (P_UPCONV + 2 * FT + c * FT))], dst[:, 1:T],
                    ALU.mult, ALU.add)))
                return nc.vector.scalar_tensor_tensor(
                    dst[:, 2:T], up_raw[c][:, 0:T - 2], par[:, at(j + (P_UPCONV + c * FT))], dst[:, 2:T],
                    ALU.mult, ALU.add)

            def up_product():
                dve.wait_ge(silu_ready, silus.add())
                nc.vector.tensor_tensor(hidden[:], silu_a[:], up_b[:], ALU.mult).then_inc(hidden_read, 1)
                used.add()

            def up_parts(j):
                dve.wait_ge(hidden_read, used.value())
                dve.wait_ge(vec_step, step(nc.vector.tensor_copy(flat(hid_h, j), hidden[:])))
                nc.vector.tensor_tensor(flat(hid_l, j), hidden[:], flat(hid_h, j).bitcast(F32),
                                        ALU.subtract).then_inc(hidden_ready, 1)

            def up_second(j, before, slots=(0, 1)):
                scale_tokens(slots[0], up_raw[0][:])
                split(LEAD + 2 if slots == (0, 1) else LEAD + 3)
                up_taps(j, 0, up_a).then_inc(taps_made, 1)
                if slots == (0, 1):
                    split(LEAD + 3)
                up_parts(before)
                scale_tokens(slots[1], up_raw[1][:])

            def up_pair(j):
                split(LEAD)
                dve.wait_ge(vec_step, step(up_taps(j - 1, 1, up_b)))
                split(LEAD + 1)
                up_product()
                up_second(j, j - 1)

            split(LEAD + 3)
            for c in range(2):
                finished(c, 3 - 2 * c, wait=False)
            for n in range(3):
                split(LEAD + n)
            reciprocal_root()
            for c in range(2):
                dve.wait_ge(acc_read[c], reads[c].value())
                nc.vector.tensor_tensor(up_raw[c][:], up_raw[c][:], rstd[:], ALU.mult).then_inc(up_scaled, 1)
            dve.wait_ge(up_scaled, 2)
            up_taps(0, 0, up_a).then_inc(taps_made, 1)
            dve.wait_ge(vec_step, step(up_taps(0, 1, up_b)))
            up_product()
            up_second(1, 0, (2, 3))
            with loop(FT - 2, 2, [0, 1], {steps: 4, taps: 2, silus: 1, used: 1}) as j:
                up_pair(j + 2)

            def down_pair(first, last):
                for c in range(2):
                    for n in range(DOWN_SLABS):
                        m = c * DOWN_SLABS + n + LEAD
                        if not last or m < 2 * DOWN_SLABS:
                            split(m, DOWN_SIZES[m % DOWN_SLABS])
                        if first and c == 0 and n == 0:
                            dve.wait_ge(vec_step, step(up_taps(FT - 1, 1, up_b)))
                        if first and c == 0 and n == 1:
                            up_product()
                            up_parts(FT - 1)
                            dve.wait_ge(vec_step, step(nc.vector.memset(square_sum[:], 0.0)))
                    finished(c, DOWN_SLABS, wait=False)
                    add_square(c)
            down_pair(True, False)
            with repeat(dve, KT // 2 - 2, {slabs: 2 * DOWN_SLABS, cols: 2 * DOWN_SLABS, reads[0]: 1, reads[1]: 1,
                                           squares_in: 2, added: 2}):
                down_pair(False, False)
            down_pair(False, True)
            reciprocal_root()
            for a, b in PARTS_OUT:
                add_normed(down_out, down_out, a, b, out_made)

        @block.tensor
        def _(pe):
            slabs = Tally(RING)
            reads = [Tally() for _ in range(4)]
            merged, qruns, vreads, osq, diags = (Tally() for _ in range(5))
            scaled_heads = Tally(HEADS)

            def products(s, out, rhs, k, b, last_k):
                nc.tensor.matmul(out, high[s][:, b, :], rhs[0][:, k, :], start=(k == 0), stop=False)
                nc.tensor.matmul(out, high[s][:, b, :], rhs[1][:, k, :], start=False, stop=False)
                return nc.tensor.matmul(out, low[s][:, b, :], rhs[0][:, k, :], start=False, stop=(k == last_k))

            def slab(n, out, rhs, k0, size, last_k):
                pe.wait_ge(low_ready, slabs.add())
                for b in range(size):
                    done = products(n % RING, out, rhs, k0 + b, b, last_k)
                done.then_inc(slabs_used, 1)

            def col(n, slot, rhs, ready=None, extra=None):
                pe.wait_ge(acc_read[slot], reads[slot].add())
                for b in range(2):
                    if ready:
                        pe.wait_ge(ready[0], ready[1] + (b + 1) * SLAB)
                    slab(n + b, acc[slot][:, 0:T], rhs, b * SLAB, SLAB, KT - 1)
                    if extra:
                        extra(b)

            def side_by_side(parts, made):
                for slot in range(2):
                    pe.wait_ge(acc_read[slot], reads[slot].add())
                for n, (a, b) in enumerate(parts):
                    pe.wait_ge(gained_ready, made + n + 1)
                    for slot in range(2):
                        if a % SLAB == 0:
                            pe.wait_ge(low_ready, slabs.add())
                        for k in range(a, b):
                            done = products(2 * (a // SLAB) + slot, acc[slot][:, 0:T], gained_hl, k, k % SLAB, KT - 1)
                        if b % SLAB == 0:
                            done.then_inc(slabs_used, 1)

            def loop(trips, n_cols, slots, more=None):
                per = {slabs: 2 * n_cols}
                for s in range(4):
                    per[reads[s]] = slots.count(s)
                per.update(more or {})
                return repeat(pe, trips, per)

            def channel_sum():
                nc.tensor.matmul(stat_ps[:, 0:T], ones[:], square_sum[:], start=True, stop=True).then_inc(sums_made, 1)

            pe.sem_inc(slabs_used, RING)
            pe.wait_ge(consts_made, 1)

            gained_hl, conv_hl, heads_hl = (gained_h, gained_l), (conv_h, conv_l), (heads_h, heads_l)
            mixed_hl, hid_hl = (mixed_h, mixed_l), (hid_h, hid_l)

            def mean_square(n):
                def extra(b):
                    if b == 1:
                        pe.wait_ge(square_sum_made, n)
                        channel_sum()
                return extra

            side_by_side(PARTS, 0)
            for c in range(2, 6):
                col(2 * c, c % 3, gained_hl, None, mean_square(1) if c == 2 else None)
            with loop(KT // 2 - 1, 6, [0, 1, 2] * 2):
                for c in range(6):
                    col(2 * c, c % 3, gained_hl)
            with loop(KT, 2, [0, 1]):
                col(0, 0, gained_hl)
                col(2, 1, conv_hl, (conv_ready, 0))

            def score_level(s):
                if s == LEVELS:
                    done = nc.tensor.matmul(level_ps[:, 0:CHUNK], k_run[:, 0:CHUNK], q_run[:, CHUNK:T],
                                            start=True, stop=True)
                else:
                    h = 1 << s
                    q = q_run[:].rearrange("p (c b u h) -> p c b u h", c=2, u=2, h=h)
                    n = h if s == LEVELS - 1 else CHUNK
                    for c in range(2):
                        done = nc.tensor.matmul(
                            level_ps[0:n, c * 64:c * 64 + 64].rearrange("p (b h) -> p b h", h=h),
                            k_run[:, c * CHUNK:c * CHUNK + n], q[:, c, :, 1, :], start=True, stop=True)
                done.then_inc(level_scored, 1)

            def head_extras(b, c, levels_on, out_on, head):
                s = 2 * c + b
                if s == 0 and out_on:
                    pe.wait_ge(level_merged, merged.add())
                    pe.wait_ge(v_ready, vreads.add())
                    nc.tensor.matmul(o_ps[:, 0:T], v_tok[:, 0, :], scores[:, 0:2, :].rearrange("p a t -> p (a t)"), start=True, stop=False)
                    nc.tensor.matmul(o_ps[:, CHUNK:T], v_tok[:, 1, :], scores[:, 2, :], start=False, stop=True
                                     ).then_inc(o_made, 1)
                if s == 0 and levels_on:
                    pe.wait_ge(q_run_ready, qruns.add())
                    for c2 in range(2):
                        n = CHUNK + CHUNK // 2
                        done = nc.tensor.matmul(level_ps[:, CHUNK + c2 * n:CHUNK + (c2 + 1) * n],
                                                key[:, c2 * CHUNK:(c2 + 1) * CHUNK], first_q[:, c2, :],
                                                start=True, stop=True)
                    done.then_inc(level_scored, 1)
                if s == 1 and levels_on:
                    pe.wait_ge(acc_read[3], reads[3].value() + 1)
                    for c2 in range(2):
                        done = nc.tensor.transpose(v_ps[:, c2 * P:(c2 + 1) * P], v_chan[:, c2 * P:(c2 + 1) * P], ident[:])
                    done.then_inc(v_transposed, 1)
                if s > 0 and levels_on:
                    pe.wait_ge(level_merged, merged.add())
                    score_level(s)
                if s == 2 and out_on:
                    pe.wait_ge(o_squared, osq.add())
                    for half in range(2):
                        done = nc.tensor.matmul(stat_ps[:, at(head + half * HEADS)],
                                                o_square[:, half * P:(half + 1) * P], ones[:, 0:1],
                                                start=True, stop=True)
                    done.then_inc(head_summed, 1)

            def head(levels_on, out_on, i):
                for c in range(4):
                    col(2 * c, c, gained_hl, None, lambda b, c=c: head_extras(b, c, levels_on, out_on, i))

            head(False, False, None)
            head(True, False, None)
            with loop(HEADS - 2, 4, [0, 1, 2, 3], {merged: LEVELS + 1, qruns: 1, vreads: 1, osq: 1}) as i:
                head(True, True, i)
            head(True, True, HEADS - 2)
            for c in range(2):
                col(2 * c, c, gained_hl, None, lambda b, c=c: head_extras(b, c, False, True, HEADS - 1))
            for c in range(2):
                col(2 * c, c, gained_hl)
            with loop(4, 2, [0, 1], {diags: 4, scaled_heads: 4}):
                for c in range(2):
                    def spread(b, c=c):
                        h = 2 * c + b
                        pe.wait_ge(diag_ready, diags.add())
                        pe.wait_ge(head_scaled, scaled_heads.value() - 1)
                        scaled_heads.add()
                        nc.tensor.matmul(bcast_ps[h % 2][:, 0:T], ones[:], diag[h % 2][:].rearrange("p a b -> p (a b)"),
                                         start=True, stop=True).then_inc(head_bcast, 1)
                    col(2 * c, c, gained_hl, None, spread)
            with loop(KT // 2, 2, [0, 1]):
                for c in range(2):
                    col(2 * c, c, heads_hl, (heads_ready, 2))
            with loop(KT // 2, 2, [0, 1]):
                for c in range(2):
                    col(2 * c, c, mixed_hl, (mixed_ready, 0))
            pe.wait_ge(squares_read, 2 + KT)
            channel_sum()
            side_by_side(PARTS, len(PARTS))
            for c in range(2):
                col(2 * c, c + 2, gained_hl, None, mean_square(2) if c == 0 else None)
            with loop(FT - 2, 2, [0, 1]):
                for c in range(2):
                    col(2 * c, c, gained_hl)
            with repeat(pe, KT // 2, {slabs: 2 * DOWN_SLABS, reads[0]: 1, reads[1]: 1}):
                for c in range(2):
                    pe.wait_ge(acc_read[c], reads[c].add())
                    for n in range(DOWN_SLABS):
                        if n in (0, DOWN_SLABS - 1):
                            pe.wait_ge(hidden_ready, SLAB * (DOWN_SLABS - 1) if n == 0 else FT)
                        slab(c * DOWN_SLABS + n, acc[c][:, 0:T], hid_hl, n * SLAB, DOWN_SIZES[n], FT - 1)
            pe.wait_ge(squares_read, 2 + 2 * KT)
            channel_sum()


def kernel(**inputs):
    import concourse.bacc as bacc
    from concourse.bass_utils import run_bass_kernel_spmd

    a = {k: np.asarray(v) for k, v in inputs.items()}

    def slabs(w):
        n = w.shape[1] // P
        return w.reshape(KT // SLAB, SLAB, P, n, P).transpose(3, 0, 2, 1, 4)

    names = ("q", "f", "i", "g", "cb", "cc", "ch", "ga", "gb")
    w_in = slabs(a["w_in"][0])
    w = {name: w_in[n * KT:(n + 1) * KT] for n, name in enumerate(names)}
    w["sc_out"], w["hg_out"], w["mix"] = (slabs(a[n][0]) for n in ("w_sc_out", "w_hg_out", "w_mix_out"))
    up = slabs(a["w_ffn_up"][0])
    w["up_a"], w["up_b"] = up[:FT], up[FT:]
    w_main = np.empty((COLS_MAIN, KT // SLAB, P, SLAB, P), np.float32)
    start = 0
    for group in (("cc", "ch", "cb"), ("gb", "sc_out"), ("f", "q", "g", "i"), ("ga",), ("hg_out",), ("mix",),
                  ("up_a", "up_b")):
        n = len(w[group[0]])
        for m, name in enumerate(group):
            w_main[start + m:start + n * len(group):len(group)] = w[name]
        if len(group) == 3 or name == "up_b":
            w_main[start:start + 2] = w_main[start:start + 2].swapaxes(0, 1).reshape(w_main[:2].shape)
        start += n * len(group)
    w_main = w_main.reshape(SLABS_MAIN, P, SLAB, P)
    w_down = np.ascontiguousarray(a["w_ffn_down"][0].reshape(FT, P, KT, P).transpose(2, 1, 0, 3))

    def channels(v):
        return v.reshape(-1, P).T

    params = np.ascontiguousarray(np.concatenate([channels(v) for v in (
        a["norm_mix_pre"][0], a["norm_mix_post"][0], a["norm_ffn_pre"][0], a["norm_ffn_post"][0],
        a["hg_lower_bounds"][0], a["hg_out_norm"][0], a["sc_conv"][0], a["ffn_conv"][0], a["ffn_conv_bias"][0])], axis=1))

    def tiles(v):
        return np.ascontiguousarray(v.T.reshape(KT, P, T).transpose(1, 0, 2))

    ident = np.eye(P, dtype=np.float32)
    masks = np.zeros((P, LEVELS, CHUNK // 2), np.float32)
    for lv in range(LEVELS):
        h = 1 << lv
        for s in range(P):
            if s % (2 * h) < h:
                b = s // (2 * h)
                masks[s, lv, b * h:(b + 1) * h] = 1

    nc = bacc.Bacc("TRN2", target_bir_lowering=False, num_devices=1)
    arrays = {"xT": tiles(a["x"][0]), "params": params, "ident_c": ident, "masks_c": masks,
              "w_main": w_main, "w_down": w_down}
    aps = [nc.dram_tensor(n, list(v.shape), mybir.dt.from_np(v.dtype), kind="ExternalInput").ap() for n, v in arrays.items()]
    out = nc.dram_tensor("outT", [P, KT, T], F32, kind="ExternalOutput").ap()
    build(nc, *aps, out)
    r = run_bass_kernel_spmd(nc, [arrays], core_ids=[0])
    y = np.asarray(r.results[0]["outT"])
    return np.ascontiguousarray(y.transpose(2, 1, 0).reshape(1, T, D_MODEL))
```
